# Optimizing a Trainium2 kernel written in Bass

```python
import math
import jax, jax.numpy as jnp
from jax import lax
import numpy as np

D_MODEL = 1024
BATCH = 1
SEQ = 512
DEPTH = 2
DEC_BATCH = 8
DEC_SEQ = 4
PAST_LEN = 2048
PAGE_SIZE = 128

N_GLA = (DEPTH + 1) // 2
N_MLA = DEPTH // 2
ALPHA = (2.0 * DEPTH) ** 0.25
BETA = (8.0 * DEPTH) ** -0.25
LN_EPS = 1e-5
RMS_EPS = 1e-6
NEG_INF = -1e30
GLA_HEADS = 4
GLA_DK = D_MODEL // 2 // GLA_HEADS
GLA_DV = D_MODEL // GLA_HEADS
GLA_GATE_RANK = 16
GLA_TAU = 16.0
GLA_CHUNK = 64
GLA_IN = 2 * GLA_HEADS * GLA_DK + 2 * GLA_HEADS * GLA_DV + GLA_GATE_RANK
MLA_HEADS = D_MODEL // 128
MLA_D_NOPE = 128
MLA_D_ROPE = 64
MLA_D_V = 128
MLA_Q_LORA = 3 * D_MODEL // 4
MLA_KV_LORA = D_MODEL // 4
MLA_IN = MLA_Q_LORA + MLA_KV_LORA + MLA_D_ROPE
ROPE_THETA = 10000.0
Q_BLOCK = 128
PEER_HEADS = 8
PEER_N_KEYS = 128
PEER_N_EXPERTS = PEER_N_KEYS ** 2
PEER_TOPK = 16
PEER_D_QUERY = 256
PEER_BLOCK = 128

kernel_name = 'hybrid_gla_mla_peer_step'

def _standardize(x):
    xf = x.astype(jnp.float32)
    mu = jnp.mean(xf, axis=-1, keepdims=True)
    var = jnp.mean(jnp.square(xf - mu), axis=-1, keepdims=True)
    return (xf - mu) * lax.rsqrt(var + LN_EPS)

def layer_norm(x, g, b):
    return (_standardize(x) * g.astype(jnp.float32) + b.astype(jnp.float32)).astype(x.dtype)

def rms_norm(x, g):
    xf = x.astype(jnp.float32)
    y = xf * lax.rsqrt(jnp.mean(jnp.square(xf), axis=-1, keepdims=True) + RMS_EPS)
    return (y * g.astype(jnp.float32)).astype(x.dtype)

def rope_angles(pos):
    half = MLA_D_ROPE // 2
    inv_freq = ROPE_THETA ** (-jnp.arange(half, dtype=jnp.float32) / half)
    return pos.astype(jnp.float32)[:, None] * inv_freq[None, :]

def apply_rope(x, ang):
    half = x.shape[-1] // 2
    xf = x.astype(jnp.float32)
    x1, x2 = xf[..., :half], xf[..., half:]
    c, s = jnp.cos(ang), jnp.sin(ang)
    return jnp.concatenate([x1 * c - x2 * s, x1 * s + x2 * c], axis=-1).astype(x.dtype)

def gla_recurrence(q, k, v, g, s0):
    B, T, H, DK = q.shape
    DV = v.shape[-1]
    C = math.gcd(T, GLA_CHUNK)
    N = T // C
    f32 = jnp.float32
    q, k, v, g = (a.astype(f32).reshape(B, N, C, H, a.shape[-1]) for a in (q, k, v, g))
    b = jnp.cumsum(g, axis=2)
    b_last = b[:, :, -1]
    qd = q * jnp.exp(b)
    kd = k * jnp.exp(-b)
    ke = k * jnp.exp(b_last[:, :, None] - b)
    causal = jnp.tril(jnp.ones((C, C), dtype=bool))
    att = jnp.where(causal, jnp.einsum('bnthk,bnshk->bnhts', qd, kd), 0.0)
    o_intra = jnp.einsum('bnhts,bnshv->bnthv', att, v)
    d_state = jnp.einsum('bnshk,bnshv->bnhkv', ke, v)

    def step(s, inp):
        log_decay, ds = inp
        return jnp.exp(log_decay)[..., None] * s + ds, s

    s_fin, s_start = lax.scan(step, s0.astype(f32),
                              (jnp.swapaxes(b_last, 0, 1), jnp.swapaxes(d_state, 0, 1)))
    o_inter = jnp.einsum('bnthk,nbhkv->bnthv', qd, s_start)
    return (o_intra + o_inter).reshape(B, T, H, DV), s_fin

def gla_mixer(h, s0, w_in, w_g2, b_g, norm_g, w_o):
    B, T, _ = h.shape
    hk, hv = GLA_HEADS * GLA_DK, GLA_HEADS * GLA_DV
    q, k, v, r, gl = jnp.split(h @ w_in, [hk, 2 * hk, 2 * hk + hv, 2 * hk + 2 * hv], axis=-1)
    log_a = jax.nn.log_sigmoid((gl @ w_g2 + b_g).astype(jnp.float32)) / GLA_TAU
    heads = lambda a: a.reshape(B, T, GLA_HEADS, -1)
    o, s_fin = gla_recurrence(heads(q) * (GLA_DK ** -0.5), heads(k), heads(v), heads(log_a), s0)
    o = (_standardize(o) * norm_g.astype(jnp.float32)).astype(h.dtype).reshape(B, T, hv)
    return (o * jax.nn.silu(r)) @ w_o, s_fin.astype(s0.dtype)

def latent_attention(q_lat, q_rope, k_lat, k_rope, q_pos, k_pos):
    B, T, H, DC = q_lat.shape
    qb = math.gcd(T, Q_BLOCK)
    nb = T // qb
    scale = (MLA_D_NOPE + MLA_D_ROPE) ** -0.5

    def block(args):
        ql, qr, qp = args
        s = (jnp.einsum('bqhc,bkc->bhqk', ql, k_lat).astype(jnp.float32)
             + jnp.einsum('bqhr,bkr->bhqk', qr, k_rope).astype(jnp.float32)) * scale
        s = jnp.where(k_pos[None, :] <= qp[:, None], s, NEG_INF)
        p = jax.nn.softmax(s, axis=-1).astype(k_lat.dtype)
        return jnp.einsum('bhqk,bkc->bqhc', p, k_lat)

    split = lambda a: jnp.swapaxes(a.reshape(B, nb, qb, H, a.shape[-1]), 0, 1)
    out = lax.map(block, (split(q_lat), split(q_rope), q_pos.reshape(nb, qb)))
    return jnp.swapaxes(out, 0, 1).reshape(B, T, H, DC)

def mla_mixer(h, past_ckv, past_kr, w_in, g_q, g_kv, w_uq, w_uk, w_uv, w_o):
    B, T, _ = h.shape
    P = past_ckv.shape[1]
    cq, ckv, kr = jnp.split(h @ w_in, [MLA_Q_LORA, MLA_Q_LORA + MLA_KV_LORA], axis=-1)
    q = (rms_norm(cq, g_q) @ w_uq).reshape(B, T, MLA_HEADS, MLA_D_NOPE + MLA_D_ROPE)
    q_nope, q_rope = q[..., :MLA_D_NOPE], q[..., MLA_D_NOPE:]
    pos = P + jnp.arange(T, dtype=jnp.int32)
    ang = rope_angles(pos)
    q_rope = apply_rope(q_rope, ang[None, :, None, :])
    kr = apply_rope(kr, ang[None])
    ckv = rms_norm(ckv, g_kv)
    q_lat = jnp.einsum('bthn,chn->bthc', q_nope, w_uk)
    keys_c = jnp.concatenate([past_ckv.astype(ckv.dtype), ckv], axis=1)
    keys_r = jnp.concatenate([past_kr.astype(kr.dtype), kr], axis=1)
    o_lat = latent_attention(q_lat, q_rope, keys_c, keys_r, pos,
                             jnp.arange(P + T, dtype=jnp.int32))
    o = jnp.einsum('bthc,chv->bthv', o_lat, w_uv).reshape(B, T, MLA_HEADS * MLA_D_V)
    return o @ w_o, ckv, kr

def peer(h, w_q, sub_k1, sub_k2, emb_u, emb_v):
    B, T, D = h.shape
    n = B * T
    x = h.reshape(n, D)
    q = _standardize((x @ w_q).reshape(n, PEER_HEADS, PEER_D_QUERY))
    half = PEER_D_QUERY // 2
    s1 = jnp.einsum('nhd,kd->nhk', q[..., :half], sub_k1.astype(jnp.float32))
    s2 = jnp.einsum('nhd,kd->nhk', q[..., half:], sub_k2.astype(jnp.float32))
    v1, i1 = lax.top_k(s1, PEER_TOPK)
    v2, i2 = lax.top_k(s2, PEER_TOPK)
    n_cand = PEER_TOPK * PEER_TOPK
    cand_s = (v1[..., :, None] + v2[..., None, :]).reshape(n, PEER_HEADS, n_cand)
    cand_i = (i1[..., :, None] * PEER_N_KEYS + i2[..., None, :]).reshape(n, PEER_HEADS, n_cand)
    top_s, top_j = lax.top_k(cand_s, PEER_TOPK)
    expert = jnp.take_along_axis(cand_i, top_j, axis=-1)
    gate = jax.nn.softmax(top_s, axis=-1).astype(h.dtype)
    blk = math.gcd(n, PEER_BLOCK)
    nb = n // blk

    def block(args):
        xb, eb, gb = args
        act = jax.nn.gelu(jnp.einsum('nd,nhkd->nhk', xb, emb_u[eb]), approximate=False) * gb
        return jnp.einsum('nhk,nhkd->nd', act, emb_v[eb])

    out = lax.map(block, (x.reshape(nb, blk, D),
                          expert.reshape(nb, blk, PEER_HEADS, PEER_TOPK),
                          gate.reshape(nb, blk, PEER_HEADS, PEER_TOPK)))
    return out.reshape(B, T, D)

def trunk(x, c, gla_init, mla_past, p):
    new_gla, new_ckv, new_kr = [], [], []
    cond = jax.nn.silu(c)
    for l in range(DEPTH):
        j = l // 2
        mod = (cond @ p['ada_w'][l] + p['ada_b'][l])[:, None, :]
        shift1, scale1, gate1, shift2, scale2, gate2 = jnp.split(mod, 6, axis=-1)
        hm = x * (1 + scale1) + shift1
        if l % 2 == 0:
            out, s_fin = gla_mixer(hm, gla_init[j], p['gla_w_in'][j], p['gla_w_g2'][j],
                                   p['gla_b_g'][j], p['gla_norm_g'][j], p['gla_w_o'][j])
            new_gla.append(s_fin)
        else:
            out, ckv, kr = mla_mixer(hm, mla_past[j][0], mla_past[j][1], p['mla_w_in'][j],
                                     p['mla_g_q'][j], p['mla_g_kv'][j], p['mla_w_uq'][j],
                                     p['mla_w_uk'][j], p['mla_w_uv'][j], p['mla_w_o'][j])
            new_ckv.append(ckv)
            new_kr.append(kr)
        x = layer_norm(ALPHA * x + gate1 * out, p['ln_g'][l, 0], p['ln_b'][l, 0])
        hf = x * (1 + scale2) + shift2
        ffn = peer(hf, p['peer_w_q'][l], p['peer_k1'][l], p['peer_k2'][l],
                   p['peer_u'][l], p['peer_v'][l])
        x = layer_norm(ALPHA * x + gate2 * ffn, p['ln_g'][l, 1], p['ln_b'][l, 1])
    return x, jnp.stack(new_gla), jnp.stack(new_ckv), jnp.stack(new_kr)

def setup_inputs(seed: int = 0) -> dict:
    key = jax.random.key(seed)
    ks = jax.random.split(key, 29)

    def nrm(k, shape, scale=1.0):
        return jax.random.normal(k, shape, jnp.float32) * scale

    n_pages = PAST_LEN // PAGE_SIZE
    n_pool = (DEC_BATCH * n_pages * 5) // 4
    hk, hv = GLA_HEADS * GLA_DK, GLA_HEADS * GLA_DV
    v_cols = jnp.ones((GLA_IN,), jnp.float32).at[2 * hk:2 * hk + hv].set(BETA)
    page_table = jax.random.permutation(ks[7], n_pool)[:DEC_BATCH * n_pages]
    page_table = page_table.reshape(DEC_BATCH, n_pages).astype(jnp.int32)
    d = D_MODEL
    return {
        'x_prompt': nrm(ks[0], (BATCH, SEQ, d)),
        'x_sample': nrm(ks[1], (DEC_BATCH, DEC_SEQ, d)),
        'c_prompt': nrm(ks[2], (BATCH, d)),
        'c_sample': nrm(ks[3], (DEC_BATCH, d)),
        'cache_ckv': nrm(ks[4], (N_MLA, n_pool, PAGE_SIZE, MLA_KV_LORA)),
        'cache_krope': nrm(ks[5], (N_MLA, n_pool, PAGE_SIZE, MLA_D_ROPE)),
        'state_gla': nrm(ks[6], (N_GLA, DEC_BATCH, GLA_HEADS, GLA_DK, GLA_DV), 0.5),
        'page_table': page_table,
        'ada_w': nrm(ks[8], (DEPTH, d, 6 * d), d ** -0.5),
        'ada_b': nrm(ks[9], (DEPTH, 6 * d), 0.02),
        'ln_g': 1.0 + nrm(ks[10], (DEPTH, 2, d), 0.02),
        'ln_b': nrm(ks[11], (DEPTH, 2, d), 0.02),
        'gla_w_in': nrm(ks[12], (N_GLA, d, GLA_IN), d ** -0.5) * v_cols,
        'gla_w_g2': nrm(ks[13], (N_GLA, GLA_GATE_RANK, hk), GLA_GATE_RANK ** -0.5),
        'gla_b_g': nrm(ks[14], (N_GLA, hk), 0.1),
        'gla_norm_g': 1.0 + nrm(ks[15], (N_GLA, GLA_DV), 0.02),
        'gla_w_o': nrm(ks[16], (N_GLA, hv, d), BETA * hv ** -0.5),
        'mla_w_in': nrm(ks[17], (N_MLA, d, MLA_IN), d ** -0.5),
        'mla_g_q': 1.0 + nrm(ks[18], (N_MLA, MLA_Q_LORA), 0.02),
        'mla_g_kv': 1.0 + nrm(ks[19], (N_MLA, MLA_KV_LORA), 0.02),
        'mla_w_uq': nrm(ks[20], (N_MLA, MLA_Q_LORA, MLA_HEADS * (MLA_D_NOPE + MLA_D_ROPE)), MLA_Q_LORA ** -0.5),
        'mla_w_uk': nrm(ks[21], (N_MLA, MLA_KV_LORA, MLA_HEADS, MLA_D_NOPE), MLA_KV_LORA ** -0.5),
        'mla_w_uv': nrm(ks[22], (N_MLA, MLA_KV_LORA, MLA_HEADS, MLA_D_V), BETA * MLA_KV_LORA ** -0.5),
        'mla_w_o': nrm(ks[23], (N_MLA, MLA_HEADS * MLA_D_V, d), BETA * (MLA_HEADS * MLA_D_V) ** -0.5),
        'peer_w_q': nrm(ks[24], (DEPTH, d, PEER_HEADS * PEER_D_QUERY), d ** -0.5),
        'peer_k1': nrm(ks[25], (DEPTH, PEER_N_KEYS, PEER_D_QUERY // 2), (PEER_D_QUERY // 2) ** -0.5),
        'peer_k2': nrm(ks[26], (DEPTH, PEER_N_KEYS, PEER_D_QUERY // 2), (PEER_D_QUERY // 2) ** -0.5),
        'peer_u': nrm(ks[27], (DEPTH, PEER_N_EXPERTS, d), d ** -0.5),
        'peer_v': nrm(ks[28], (DEPTH, PEER_N_EXPERTS, d), BETA),
    }

def reference(x_prompt, x_sample, c_prompt, c_sample, cache_ckv, cache_krope, state_gla,
              page_table, ada_w, ada_b, ln_g, ln_b, gla_w_in, gla_w_g2, gla_b_g, gla_norm_g,
              gla_w_o, mla_w_in, mla_g_q, mla_g_kv, mla_w_uq, mla_w_uk, mla_w_uv, mla_w_o,
              peer_w_q, peer_k1, peer_k2, peer_u, peer_v):
    p = dict(ada_w=ada_w, ada_b=ada_b, ln_g=ln_g, ln_b=ln_b, gla_w_in=gla_w_in,
             gla_w_g2=gla_w_g2, gla_b_g=gla_b_g, gla_norm_g=gla_norm_g, gla_w_o=gla_w_o,
             mla_w_in=mla_w_in, mla_g_q=mla_g_q, mla_g_kv=mla_g_kv, mla_w_uq=mla_w_uq,
             mla_w_uk=mla_w_uk, mla_w_uv=mla_w_uv, mla_w_o=mla_w_o, peer_w_q=peer_w_q,
             peer_k1=peer_k1, peer_k2=peer_k2, peer_u=peer_u, peer_v=peer_v)
    dt = x_prompt.dtype
    bp = x_prompt.shape[0]
    gla_zero = [jnp.zeros((bp, GLA_HEADS, GLA_DK, GLA_DV), dt) for _ in range(N_GLA)]
    no_past = [(jnp.zeros((bp, 0, MLA_KV_LORA), dt), jnp.zeros((bp, 0, MLA_D_ROPE), dt))
               for _ in range(N_MLA)]
    y_prompt, gla_prompt, ckv_prompt, krope_prompt = trunk(x_prompt, c_prompt, gla_zero, no_past, p)
    bs, n_pages = page_table.shape
    past = [(cache_ckv[j][page_table].reshape(bs, n_pages * PAGE_SIZE, MLA_KV_LORA),
             cache_krope[j][page_table].reshape(bs, n_pages * PAGE_SIZE, MLA_D_ROPE))
            for j in range(N_MLA)]
    gla_past = [state_gla[j] for j in range(N_GLA)]
    y_sample, gla_sample, ckv_sample, krope_sample = trunk(x_sample, c_sample, gla_past, past, p)
    return (y_prompt, y_sample, gla_prompt, gla_sample, ckv_prompt, krope_prompt, ckv_sample, krope_sample)


_drawn_inputs = setup_inputs


def setup_inputs(seed=0):
    import zlib

    import numpy as np

    out = dict(_drawn_inputs(seed))
    spreads = {}
    factors = {'cache_ckv': 5.674,
     'cache_krope': 8.0,
     'gla_norm_g': 3.27,
     'mla_g_q': 8.0,
     'mla_g_kv': 2.827,
     'mla_w_uq': 2.813,
     'mla_w_uk': 3.135}
    for name, (base, spread) in spreads.items():
        noise = np.random.default_rng([zlib.crc32(name.encode()), seed]).standard_normal(out[name].shape)
        drawn = base * np.exp(spread * noise) if base else spread * noise
        out[name] = __import__('jax').numpy.asarray(drawn.astype(out[name].dtype))
    for name, factor in factors.items():
        out[name] = (out[name] * factor).astype(out[name].dtype)
    return out
```

```python
import numpy as np
import concourse.bass as bass
from concourse import mybir
from contextlib import ExitStack

F32 = mybir.dt.float32
I32 = mybir.dt.int32
U32 = mybir.dt.uint32
ALU = mybir.AluOpType
ACT = mybir.ActivationFunctionType
AX = mybir.AxisListType.X

P = 128
D = 1024
KC = D // P
SEQ, DEC_B, DEC_T, PAST, PAGE = 512, 8, 4, 2048, 128
NS_TOK = DEC_B * DEC_T
N = SEQ + NS_TOK
HALF = N // 2
TILES = [(i, P) for i in range(SEQ // P)] + [(SEQ // P, NS_TOK)]
NT = len(TILES)
NSEQ = 1 + DEC_B
ALPHA = 4.0 ** 0.25
LN_EPS, RMS_EPS, NEG = 1e-5, 1e-6, -1e30
GH, GDK, GDV, GCH, GTAU = 4, 128, 256, 64, 16.0
NCHUNK = SEQ // GCH
MH, QLORA, KVL, DR, DN = 8, 768, 256, 64, 128
QC = QLORA // P
MSCALE = float(DN + DR) ** -0.5
PH, NK, TOPK = 8, 128, 16
RING = 8
SLOT = 1024
TPG = 4
NBLK = N // 32
NPAGE = PAST // PAGE
HPAGES = NPAGE // 2

CONST = {}


def const_layout():
    at, out = 0, {}
    for name, n in (("ident", P), ("iota", P), ("chunk", P), ("chunk_s", NS_TOK), ("seqsel", DEC_B),
                    ("causal", P), ("causal_s", DEC_T)):
        out[name] = (at, n)
        at += n
    return out, at


def constants():
    lay, n = const_layout()
    c = np.zeros((P, n), np.float32)
    p, j = np.arange(P)[:, None], np.arange(P)[None, :]
    put = lambda name, v: c.__setitem__((slice(0, v.shape[0]), slice(lay[name][0], sum(lay[name]))), v)
    put("ident", np.eye(P, dtype=np.float32))
    put("iota", np.broadcast_to(j, (P, P)).astype(np.float32))
    put("chunk", ((p <= j) & (p // GCH == j // GCH)).astype(np.float32))
    ps, js = p[:NS_TOK], j[:, :NS_TOK]
    put("chunk_s", ((ps <= js) & (ps // DEC_T == js // DEC_T)).astype(np.float32))
    put("seqsel", (ps // DEC_T == j[:, :DEC_B]).astype(np.float32))
    put("causal", np.where(j <= p, 0.0, NEG).astype(np.float32))
    put("causal_s", np.where(j[:, :DEC_T] <= ps % DEC_T, 0.0, NEG).astype(np.float32))
    half = DR // 2
    inv = np.float32(10000.0) ** (-np.arange(half, dtype=np.float32) / np.float32(half))
    pos = np.concatenate([np.arange(SEQ), PAST + np.arange(NS_TOK) % DEC_T]).astype(np.float32)
    ang = (pos[:, None] * inv[None, :]).astype(np.float32)
    cos, sin = np.cos(ang).astype(np.float32), np.sin(ang).astype(np.float32)
    ct, st = np.zeros((NT * P, DR), np.float32), np.zeros((NT * P, DR), np.float32)
    ct[:N] = np.concatenate([cos, cos], 1)
    st[:N] = np.concatenate([-sin, sin], 1)
    rope_tok = np.stack([ct.reshape(NT, P, DR), st.reshape(NT, P, DR)]).transpose(2, 0, 1, 3).reshape(P, -1)
    cf = np.concatenate([cos.T] * 4, 0)
    sf = np.concatenate([sin.T, -sin.T] * 2, 0)
    rope_feat = np.concatenate([cf, sf], 1)
    return c, np.ascontiguousarray(rope_tok), np.ascontiguousarray(rope_feat)


class Steps:

    def __init__(self, eng, sem):
        self.eng, self.sem, self.n = eng, sem, 0

    def __call__(self, ins):
        self.n = self.n + 1
        ins.then_inc(self.sem, 1)
        self.eng.wait_ge(self.sem, self.n)


class Mark:

    def __init__(self, sem, base):
        self.sem, self.base = sem, base

    def __call__(self, n):
        return self.sem, n + self.base


class Ring:

    def __init__(self, buf, landed, used):
        self.buf, self.landed, self.used = buf, landed, used
        self.loaded = self.taken = 0

    def load(self, sp, src):
        n = self.loaded
        if n >= RING:
            sp.wait_ge(self.used, n - RING + 1)
        sp.dma_start(self.buf[:, n % RING, 0:src.shape[-1]], src).then_inc(self.landed[n % RING], 16)
        self.loaded = n + 1

    def load_loop(self, sp, srcs, first, count):
        base = self.loaded
        assert base >= RING or first >= 1
        with sp.Fori(first, count) as i:
            for j in range(RING):
                n = base + j
                sp.wait_ge(self.used, (i - first) * RING + (n - RING + 1))
                sp.dma_start(self.buf[:, n % RING, :], srcs(i, j)).then_inc(self.landed[n % RING], 16)
        self.loaded = base + (count - first) * RING

    def take(self, pe, turn=None, j=0):
        n = self.taken + j
        need = 16 * (n // RING + 1)
        pe.wait_ge(self.landed[n % RING], need if turn is None else turn * 16 + need)
        if turn is None:
            self.taken = n + 1
        return self.buf[:, n % RING, :]


class Arena:

    def __init__(self, buf, width):
        self.buf, self.width, self.at = buf, width, 0

    def __call__(self, *shape, at=None):
        n = int(np.prod(shape))
        if at is not None:
            self.at = at
        a = self.buf[:, self.at:self.at + n]
        self.at += n
        assert self.at <= self.width, (self.at, self.width)
        if len(shape) == 2:
            a = a.rearrange("p (a b) -> p a b", b=shape[1])
        elif len(shape) == 3:
            a = a.rearrange("p (a b c) -> p a b c", b=shape[1], c=shape[2])
        elif len(shape) == 4:
            a = a.rearrange("p (a b c d) -> p a b c d", b=shape[1], c=shape[2], d=shape[3])
        return a


def cols(tile, np_):
    return slice(tile * P, tile * P + np_)


def build(nc, d):
    ctx = ExitStack()
    with ctx:
        sb = lambda name, w, dt=F32: ctx.enter_context(nc.sbuf_tensor(name, [P, w], dt))
        sem = lambda name: ctx.enter_context(nc.semaphore(name))
        shared = {}
        turns_taken = sem("turns_taken")

        def alone(e):
            e.sem_inc(turns_taken, 1)

        def mark(name, per_use):
            handle, uses = shared.get(name, (None, 0))
            handle = handle or sem(name)
            shared[name] = (handle, uses + 1)
            return Mark(handle, uses * per_use)

        ring_buf = sb("ring", RING * SLOT)[:, :].rearrange("p (s c) -> p s c", c=SLOT)
        x = sb("x", NT * D)[:, :].rearrange("p (t c) -> p t c", c=D)
        hT = sb("hT", KC * N)[:, :].rearrange("p (k n) -> p k n", n=N)
        modT = sb("modT", 2 * 4 * KC * NSEQ)[:, :].rearrange("p (l w k s) -> p l w k s", l=2, w=4, s=NSEQ)
        lay, ncon = const_layout()
        con = sb("con", ncon)
        arena_w = 34200
        arena_buf = sb("arena", arena_w)
        ps = ctx.enter_context(nc.psum_tensor("ps", [P, 8, 512], F32))
        K = {name: con[:, a:a + n] for name, (a, n) in lay.items()}
        ident = K["ident"]

        ring = Ring(ring_buf, [sem(f"slot{i}_landed") for i in range(RING)], sem("slots_used"))
        used = ring.used
        con_in, x_in, stage_over = sem("con_in"), sem("x_in"), sem("stage_over")
        dve_chain = Steps(nc.vector, sem("dve_step"))
        stages, plan = [], [0]

        def reserve(n):
            plan[0] += n
            return plan[0] - n

        def transpose(pe, out, in_):
            return pe.transpose(out, in_, ident[0:in_.shape[0], 0:in_.shape[0]])

        def row_tiles(slot, k0, pe, src, np_cols, start, stop, bank_of, before=None, width=512):
            per = SLOT // width if width == 512 else KC
            for kk in range(per):
                k = k0 + kk
                for t, np_ in TILES:
                    if before is not None and k == 0:
                        before(t)
                    mm = pe.matmul(ps[0:np_, bank_of(t), 0:width], src[:, k, cols(t, np_)],
                                   slot[:, kk * width:(kk + 1) * width], start=(k == 0), stop=(k == KC - 1))
            mm.then_inc(used, 1)

        def pair(b):
            return ps[:, b:b + 2, 0:HALF]

        def halves(a):
            return a.rearrange("p (h n) -> p h n", h=2)

        def stage_ada():
            A = Arena(arena_buf, arena_w)
            G6 = 12
            rows, bias = A(G6 * D), A(G6 * D)
            cT = A(KC, NSEQ)
            condT = A(KC, NSEQ)
            base = reserve(G6 * RING)
            c_in, bias_in, cond_ready = sem("c_in"), sem("ada_bias_in"), sem("cond_ready")
            row_done, rows_saved = sem("mod_row_done"), sem("mod_rows_saved")
            colT_ps, colT_done = sem("modT_ps"), sem("modT_done")

            def sp(e):
                e.dma_start(con[:, :], d["con"]).then_inc(con_in, 16)
                e.dma_start(cT, d["cT"]).then_inc(c_in, 16)
                for j in range(RING):
                    ring.load(e, d["ada_w"][j])
                for t, np_ in TILES:
                    e.dma_start(x[0:np_, t, :], d["x"][t * P:t * P + np_, :]).then_inc(x_in, 16)
                ring.load_loop(e, lambda i, j: d["ada_w"][i * RING + j], 1, G6)

            def pool(e):
                e.dma_start(bias[0:NSEQ], d["ada_b"].broadcast_to([NSEQ, G6 * D])).then_inc(bias_in, 16)
                e.wait_ge(row_done, G6 + 2)
                e.dma_start(d["mod"], rows[0:NSEQ]).then_inc(rows_saved, 16)
                e.wait_ge(rows_saved, 16)

            def act(e):
                e.wait_ge(c_in, 16)
                e.activation(condT, cT, ACT.Silu).then_inc(cond_ready, 1)

            def pe(e):
                e.wait_ge(cond_ready, 1)
                with e.Fori(0, G6 // 2) as i:
                    for u in range(2):
                        e.wait_ge(row_done, i * 2 + (u + 1))
                        for k in range(KC):
                            n = u * RING + k
                            e.wait_ge(ring.landed[k], i * 32 + 16 * (u + 1))
                            for h in range(2):
                                mm = e.matmul(ps[0:NSEQ, 2 * u + h, :], condT[:, k, :],
                                              ring_buf[:, k, h * 512:(h + 1) * 512], start=(k == 0), stop=(k == KC - 1))
                            mm.then_inc(used, 1)
                ring.taken = G6 * RING
                e.wait_ge(row_done, G6 + 2)
                e.wait_ge(con_in, 16)
                for l in range(2):
                    for w, q in enumerate((0, 1, 3, 4)):
                        for k in range(KC):
                            o = (w * KC + k) * NSEQ
                            src = (l * 6 + q) * D + k * P
                            mm = transpose(e, ps[:, 4 + l, o:o + NSEQ], rows[0:NSEQ, src:src + P])
                    mm.then_inc(colT_ps, 1)

            def dve(e):
                e.wait_ge(bias_in, 16)
                e.sem_inc(row_done, 2)
                with e.Fori(0, G6 // 2) as i:
                    for u in range(2):
                        e.wait_ge(used, i * 16 + 8 * (u + 1))
                        o = bass.ds((i * 2 + u) * D, D)
                        e.tensor_tensor(rows[0:NSEQ, o], ps[0:NSEQ, 2 * u:2 * u + 2, :].rearrange("p a b -> p (a b)"),
                                        bias[0:NSEQ, o], ALU.add).then_inc(row_done, 1)
                for l in range(2):
                    e.wait_ge(colT_ps, l + 1)
                    v = ps[:, 4 + l, 0:4 * KC * NSEQ].rearrange("p (w r) -> p w r", w=4)
                    o = modT[:, l].rearrange("p w k s -> p w (k s)")
                    e.tensor_copy(o[:, 0:4:2], v[:, 0:4:2]).then_inc(colT_done, 1)
                    e.tensor_scalar(o[:, 1:4:2], v[:, 1:4:2], 1.0, None, ALU.add).then_inc(colT_done, 1)

            return sp, pe, act, dve, pool

        def stage_modulate(l, which):
            A = Arena(arena_buf, arena_w)
            tmp = A(KC, DEC_B, DEC_T)
            xT_ps, hT_done, tmp_done = mark("xT_ps", KC + 1), mark("hT_done", KC), mark("hT_tmp", 2)
            shift, scale = modT[:, l, 2 * which], modT[:, l, 2 * which + 1]

            def sp(e):
                pass

            def pe(e):
                e.wait_ge(x_in, 16 * NT)
                for k in range(KC):
                    if k >= 4:
                        e.wait_ge(*hT_done(k - 3))
                    for t in range(4):
                        mm = transpose(e, ps[:, k % 4, t * P:(t + 1) * P], x[:, t, k * P:(k + 1) * P])
                    mm.then_inc(xT_ps.sem, 1)
                for k in range(KC):
                    mm = transpose(e, ps[:, 4, k * NS_TOK:(k + 1) * NS_TOK], x[0:NS_TOK, 4, k * P:(k + 1) * P])
                mm.then_inc(xT_ps.sem, 1)

            def act(e):
                for k in range(KC):
                    e.wait_ge(*xT_ps(k + 1))
                    e.activation(hT[:, k, 0:SEQ], ps[:, k % 4, :], ACT.Identity,
                                 bias=shift[:, k, 0:1], scale=scale[:, k, 0:1]).then_inc(hT_done.sem, 1)

            def dve(e):
                e.wait_ge(*xT_ps(KC + 1))
                v = ps[:, 4, 0:KC * NS_TOK].rearrange("p (k s t) -> p k s t", k=KC, t=DEC_T)
                spread = lambda m: m[:, :, 1:].unsqueeze(3).broadcast_to([P, KC, DEC_B, DEC_T])
                e.tensor_tensor(tmp, v, spread(scale), ALU.mult).then_inc(tmp_done.sem, 1)
                e.wait_ge(*tmp_done(1))
                o = hT[:, :, SEQ:N].rearrange("p k (s t) -> p k s t", t=DEC_T)
                e.tensor_tensor(o, tmp, spread(shift), ALU.add).then_inc(tmp_done.sem, 1)

            return sp, pe, act, dve, lambda e: None

        def stage_close(l, which, w_o=None, yT=None):
            A = Arena(arena_buf, arena_w)
            if yT is not None:
                A.at = KC * N
            gate = A(2, D)
            lng, lnb = A(D), A(D)
            z = A(2, 512)
            st, mv = A(NT, 2, 6), A(NT, 2)
            var, rstd = A(NT), A(NT)
            rows_in, z_ready, var_ready, std_ready = (mark(*s) for s in (
                ("gate_rows_in", 64), ("out_gated", 2 * NT), ("var_ready", 1), ("std_ready", 1)))
            tps = mark("y_tok_ps", NT) if yT is not None else None
            base = reserve(8) if w_o is not None else 0
            y0 = (l * 6 + (5 if which else 2)) * D

            def sp(e):
                if w_o is not None:
                    for s in range(8):
                        ring.load(e, d[w_o][s])

            def pool(e):
                e.dma_start(gate[:, 0], d["mod"][0:1, y0:y0 + D].broadcast_to([P, D])).then_inc(rows_in.sem, 16)
                e.dma_start(gate[0:NS_TOK, 1], d["mod"][1:NSEQ, y0:y0 + D].unsqueeze(1).broadcast_to(
                    [DEC_B, DEC_T, D])).then_inc(rows_in.sem, 16)
                r = 2 * l + which
                e.dma_start(lng, d["ln_g"][r:r + 1, :].broadcast_to([P, D])).then_inc(rows_in.sem, 16)
                e.dma_start(lnb, d["ln_b"][r:r + 1, :].broadcast_to([P, D])).then_inc(rows_in.sem, 16)

            def pe(e):
                if w_o is not None:
                    for g in range(2):
                        for s in range(4):
                            slot = ring.take(e)
                            row_tiles(slot, 2 * s, e, hT, None, None, None, lambda t: (5 * g + t) % 8,
                                      before=(lambda t: e.wait_ge(*z_ready(t - 2)) if t >= 3 else None) if g else None)
                else:
                    for t, np_ in TILES:
                        if t == 4:
                            e.wait_ge(*z_ready(2))
                        for k in range(KC):
                            mm = transpose(e, ps[0:np_, 2 * (t % 4) + k // 4, (k % 4) * P:(k % 4 + 1) * P], yT[:, k, cols(t, np_)])
                        mm.then_inc(tps.sem, 1)

            def act(e):
                e.wait_ge(*var_ready(1))
                e.activation(rstd, var, ACT.Sqrt).then_inc(std_ready.sem, 1)

            def dve(e):
                D_ = dve_chain
                D_(e.memset(var, 1.0))
                e.wait_ge(*rows_in(64))
                items = [(g, t, np_) for g in range(2) for t, np_ in TILES] if w_o is not None else \
                    [(g, t, np_) for t, np_ in TILES for g in range(2)]
                for i, (g, t, np_) in enumerate(items):
                    if w_o is not None:
                        e.wait_ge(used, base + 4 * (g + 1))
                        b = (5 * g + t) % 8
                    else:
                        e.wait_ge(*tps(t + 1))
                        b = 2 * (t % 4) + g
                    c = slice(g * 512, (g + 1) * 512)
                    e.tensor_tensor(z[0:np_, i % 2], ps[0:np_, b, :], gate[0:np_, t // 4, c], ALU.mult).then_inc(z_ready.sem, 1)
                    e.wait_ge(*z_ready(i + 1))
                    D_(e.scalar_tensor_tensor(out=x[0:np_, t, c], in0=x[0:np_, t, c], scalar=ALPHA,
                                              in1=z[0:np_, i % 2], op0=ALU.mult, op1=ALU.add))
                for t, np_ in TILES:
                    for g in range(2):
                        e.bn_stats(st[0:np_, t, g], x[0:np_, t, g * 512:(g + 1) * 512]).then_inc(D_.sem, 1)
                        D_.n += 1
                    e.wait_ge(D_.sem, D_.n)
                    D_(e.bn_aggr(mv[0:np_, t], st[0:np_, t].rearrange("p a b -> p (a b)")))
                    D_(e.tensor_scalar(var[0:np_, t:t + 1], mv[0:np_, t, 1:2], LN_EPS, None, ALU.add))
                e.sem_inc(var_ready.sem, 1)
                e.wait_ge(*std_ready(1))
                D_(e.reciprocal(rstd, rstd))
                for t, np_ in TILES:
                    xt = x[0:np_, t]
                    D_(e.tensor_scalar(xt, xt, mv[0:np_, t, 0:1], rstd[0:np_, t:t + 1], ALU.subtract, ALU.mult))
                    D_(e.tensor_tensor(xt, xt, lng[0:np_], ALU.mult))
                    D_(e.tensor_tensor(xt, xt, lnb[0:np_], ALU.add))

            return sp, pe, act, dve, pool

        def stage_gla():
            A = Arena(arena_buf, arena_w)
            qk = A(2 * GH, N)
            expB = A(GH, N)
            Bc = A(GH, N)
            ke = A(GH, N)
            states = A(3, GH * GDV, at=qk.shape[1] * N)
            onorm = A(D)
            A.at = 5 * GH * N
            gtok = A(NT, GH * GDK)
            vtok, rtok = A(NT, D), A(NT, D)
            attT = A(2, GH * P)
            S0 = A(2, DEC_B * GDV)
            kem = A(DEC_B, GDK)
            qsel = A(GH, DEC_B * NS_TOK)
            tmpA = A(512)
            wgl = A(KC, 16)
            wg2 = A(GH * GDK)
            glT = A(N)
            normg = A(GDV)
            st, mv = A(GH, 6), A(GH, 2)
            rstd = A(GH)
            last, last_s = A(GH, NCHUNK), A(GH, DEC_B)
            base = reserve(24)
            small_in = sem("gla_small_in")
            qk_done, gl_ps, gl_done = sem("qk_done"), sem("gl_ps"), sem("gl_done")
            g_ps, lsp_done, g_done = sem("g_ps"), sem("lsp_done"), sem("g_done")
            B_ps, B_done, D_done, exp_done, kd_done = sem("B_ps"), sem("B_done"), sem("D_done"), sem("exp_done"), sem("kd_done")
            vr_done, ket_ps, ket_done = sem("vr_done"), sem("ket_ps"), sem("ket_done")
            att_ps, att_done, ds_ps, ds_done = sem("att_ps"), sem("att_done"), sem("ds_ps"), sem("ds_done")
            o_ps, o_read, ovar, ostd, on_done, oT_ps, oT_done = (sem(s) for s in (
                "o_ps", "o_read", "o_var", "o_std", "on_done", "oT_ps", "oT_done"))
            S0_in, qsel_done, kem_done, s_out = [sem("S0_in0"), sem("S0_in1")], sem("qsel_done"), sem("kem_done"), [sem("S_out0"), sem("S_out1")]
            sp_out, state_zero = sem("gla_state_out"), sem("att_zero")
            bank_vr = lambda g, t: (5 * g + t) % 8

            def sp(e):
                for s in range(24):
                    ring.load(e, d["gla_w"][s])

            def pool(e):
                e.dma_start(wgl, d["gla_wgl"]).then_inc(small_in, 16)
                e.dma_start(wg2[0:17], d["gla_wg2"]).then_inc(small_in, 16)
                e.dma_start(normg, d["gla_norm_g"].broadcast_to([P, GDV])).then_inc(small_in, 16)
                for h in range(2):
                    e.dma_start(S0[:, h].rearrange("p (b v) -> p b v", b=DEC_B), d["state_gla"][:, h].rearrange("b k v -> k b v")).then_inc(S0_in[h], 16)
                e.wait_ge(ds_done, NCHUNK)
                e.dma_start(d["o_gla_p"].rearrange("h k v -> k h v"),
                            states[:, NCHUNK % 3].rearrange("p (h v) -> p h v", h=GH)).then_inc(sp_out, 16)
                for h in range(GH):
                    e.wait_ge(ds_done, NCHUNK + 4 * (h + 1))
                    v = S0[:, h % 2].rearrange("p (b v) -> p b v", b=DEC_B)
                    e.dma_start(d["o_gla_s"][:, h].rearrange("b k v -> k b v"), v).then_inc(s_out[h % 2], 16)
                    e.wait_ge(s_out[h % 2], 16 * (h // 2 + 1))
                    if h + 2 < GH:
                        e.dma_start(v, d["state_gla"][:, h + 2].rearrange("b k v -> k b v")).then_inc(S0_in[h % 2], 16)
                e.wait_ge(sp_out, 16)

            def pe(e):
                e.wait_ge(small_in, 48)
                for m in range(2 * GH):
                    slot = ring.take(e)
                    if m >= 2:
                        e.wait_ge(qk_done, m - 1)
                    for h in range(2):
                        for k in range(KC):
                            mm = e.matmul(ps[:, 2 * (m % 2) + h, 0:HALF], slot[:, k * P:(k + 1) * P],
                                          hT[:, k, h * HALF:(h + 1) * HALF], start=(k == 0), stop=(k == KC - 1))
                    mm.then_inc(used, 1)
                for h in range(2):
                    for k in range(KC):
                        mm = e.matmul(ps[0:16, 4 + h, 0:HALF], wgl[:, k, :], hT[:, k, h * HALF:(h + 1) * HALF],
                                      start=(k == 0), stop=(k == KC - 1))
                mm.then_inc(gl_ps, 1)
                e.wait_ge(gl_done, 2)
                e.wait_ge(qk_done, 8)
                for t, np_ in TILES:
                    e.matmul(ps[0:np_, t, :], glT[0:17, cols(t, np_)], wg2[0:17], start=True, stop=True).then_inc(g_ps, 1)
                for t, np_ in TILES:
                    e.wait_ge(g_done, t + 1)
                    m = K["chunk"] if t < 4 else K["chunk_s"][0:NS_TOK]
                    for h in range(GH):
                        mm = e.matmul(ps[:, t, h * P:h * P + np_], gtok[0:np_, t, h * P:(h + 1) * P], m, start=True, stop=True)
                    mm.then_inc(B_ps, 1)
                e.wait_ge(B_done, NT)
                for g in range(4):
                    for s in range(4):
                        slot = ring.take(e)
                        row_tiles(slot, 2 * s, e, hT, None, None, None, lambda t: bank_vr(g, t),
                                  before=(lambda t: e.wait_ge(vr_done, 5 * g + t - 7) if 5 * g + t >= 8 else None))
                e.wait_ge(kd_done, 4)
                e.wait_ge(vr_done, 20)
                for t, np_ in TILES:
                    for h in range(GH):
                        mm = transpose(e, ps[0:np_, t, h * P:(h + 1) * P], ke[:, h, cols(t, np_)])
                    mm.then_inc(ket_ps, 1)
                e.wait_ge(ket_done, NT)

                def out_tile(t, np_):
                    e.wait_ge(on_done, t + 1)
                    if t:
                        e.wait_ge(oT_done, t)
                    for k in range(KC):
                        mm = transpose(e, ps[:, k // 4, (k % 4) * P:(k % 4) * P + np_], onorm[0:np_, k * P:(k + 1) * P])
                    mm.then_inc(oT_ps, 1)

                for t in range(4):
                    for h in range(GH):
                        mm = e.matmul(ps[:, 5, h * P:(h + 1) * P], qk[:, GH + h, cols(t, P)], qk[:, h, cols(t, P)], start=True, stop=True)
                    mm.then_inc(att_ps, 1)
                    for u in range(2):
                        n = 2 * t + u
                        r = slice(u * GCH, (u + 1) * GCH)
                        if n:
                            e.wait_ge(ds_done, n)
                        for h in range(GH):
                            mm = e.matmul(ps[:, 6 + h // 2, (h % 2) * GDV:(h % 2 + 1) * GDV], gtok[r, t, h * P:(h + 1) * P],
                                          vtok[r, t, h * GDV:(h + 1) * GDV], start=True, stop=True)
                        mm.then_inc(ds_ps, 1)
                    e.wait_ge(att_done, t + 1)
                    e.wait_ge(ds_done, 2 * t + 1)
                    if t:
                        e.wait_ge(o_read, t)
                    for h in range(GH):
                        o = ps[:, 2 + h // 2, (h % 2) * GDV:(h % 2 + 1) * GDV]
                        mm = e.matmul(o, attT[:, t % 2, h * P:(h + 1) * P], vtok[:, t, h * GDV:(h + 1) * GDV],
                                      start=True, stop=False, skip_group_check=True)
                        for u in range(2):
                            n = 2 * t + u
                            if n:
                                mm = e.matmul(o[u * GCH:(u + 1) * GCH], qk[:, h, n * GCH:(n + 1) * GCH],
                                              states[:, n % 3, h * GDV:(h + 1) * GDV], start=False, stop=(u == 1), skip_group_check=True)
                    mm.then_inc(o_ps, 1)
                    if t:
                        out_tile(t - 1, P)
                for h in range(GH):
                    mm = e.matmul(ps[0:NS_TOK, 5, h * P:h * P + NS_TOK], qk[:, GH + h, SEQ:N], qk[:, h, SEQ:N], start=True, stop=True)
                mm.then_inc(att_ps, 1)
                e.wait_ge(att_done, 5)
                e.wait_ge(qsel_done, 2)
                e.wait_ge(o_read, 4)
                for h in range(GH):
                    o = ps[0:NS_TOK, 2 + h // 2, (h % 2) * GDV:(h % 2 + 1) * GDV]
                    e.matmul(o, attT[0:NS_TOK, 0, h * P:h * P + NS_TOK], vtok[0:NS_TOK, 4, h * GDV:(h + 1) * GDV],
                             start=True, stop=False, skip_group_check=True)
                    e.wait_ge(S0_in[h % 2], 16 * (h // 2 + 1))
                    for b in range(DEC_B):
                        mm = e.matmul(o, qsel[:, h, b * NS_TOK:(b + 1) * NS_TOK], S0[:, h % 2, b * GDV:(b + 1) * GDV],
                                      start=False, stop=(b == DEC_B - 1), skip_group_check=True)
                    mm.then_inc(o_ps, 1)
                    e.wait_ge(kem_done, h + 1)
                    for q in range(4):
                        n = 4 * h + q
                        e.wait_ge(ds_done, NCHUNK + n - 1) if n else e.wait_ge(ds_done, NCHUNK)
                        for b in (2 * q, 2 * q + 1):
                            mm = e.matmul(ps[:, 6 + n % 2, (b % 2) * GDV:(b % 2 + 1) * GDV], kem[0:NS_TOK, b, :],
                                          vtok[0:NS_TOK, 4, h * GDV:(h + 1) * GDV], start=True, stop=True)
                        mm.then_inc(ds_ps, 1)
                    if h == 0:
                        out_tile(3, P)
                out_tile(4, NS_TOK)

            def act(e):
                S_ = Steps(e, sem("gla_act_step"))
                for m in range(2 * GH):
                    e.wait_ge(used, base + m + 1)
                    e.activation(halves(qk[:, m, :]), pair(2 * (m % 2)), ACT.Copy,
                                 scale=GDK ** -0.5 if m < GH else 1.0).then_inc(qk_done, 1)
                for t, np_ in TILES:
                    e.wait_ge(g_ps, t + 1)
                    if t:
                        e.wait_ge(g_done, t)
                    S_(e.activation(tmpA[0:np_], ps[0:np_, t, :], ACT.Abs))
                    S_(e.activation(tmpA[0:np_], tmpA[0:np_], ACT.Exp, scale=-1.0))
                    e.activation(tmpA[0:np_], tmpA[0:np_], ACT.Ln, bias=1.0).then_inc(lsp_done, 1)
                e.wait_ge(B_done, NT)
                e.activation(expB, Bc, ACT.Exp, scale=1.0 / GTAU).then_inc(exp_done, 1)
                e.wait_ge(D_done, 2)
                e.activation(ke, ke, ACT.Exp, scale=1.0 / GTAU).then_inc(exp_done, 1)
                e.activation(Bc, Bc, ACT.Exp, scale=-1.0 / GTAU).then_inc(exp_done, 1)
                for g in range(4):
                    for t, np_ in TILES:
                        e.wait_ge(used, base + 8 + 4 * (g + 1))
                        o = (vtok if g < 2 else rtok)[0:np_, t, (g % 2) * 512:(g % 2 + 1) * 512]
                        e.activation(o, ps[0:np_, bank_vr(g, t), :], ACT.Copy if g < 2 else ACT.Silu).then_inc(vr_done, 1)
                for t, np_ in TILES:
                    e.wait_ge(ovar, t + 1)
                    e.activation(rstd[0:np_], rstd[0:np_], ACT.Sqrt).then_inc(ostd, 1)
                    e.wait_ge(oT_ps, t + 1)
                    v = ps[:, 0:2, :].rearrange("p b (k n) -> p (b k) n", k=4)
                    e.activation(hT[:, :, cols(t, np_)], v[:, :, 0:np_], ACT.Copy).then_inc(oT_done, 1)

            def dve(e):
                S_ = dve_chain
                S_(e.memset(glT[0:17], 1.0))
                S_(e.memset(qsel, 0.0))
                S_(e.memset(attT, 0.0))
                e.wait_ge(gl_ps, 1)
                e.tensor_copy(halves(glT[0:16]), ps[0:16, 4:6, 0:HALF]).then_inc(gl_done, 2)
                for t, np_ in TILES:
                    e.wait_ge(lsp_done, t + 1)
                    e.scalar_tensor_tensor(out=gtok[0:np_, t], in0=ps[0:np_, t, :], scalar=0.0, in1=tmpA[0:np_],
                                           op0=ALU.min, op1=ALU.subtract).then_inc(g_done, 1)
                for t, np_ in TILES:
                    e.wait_ge(B_ps, t + 1)
                    v = ps[:, t, :].rearrange("p (h n) -> p h n", h=GH)[:, :, 0:np_]
                    e.tensor_copy(Bc[:, :, cols(t, np_)], v).then_inc(B_done, 1)
                e.wait_ge(B_done, NT)
                for a, c, w in ((0, NCHUNK, GCH), (SEQ, DEC_B, DEC_T)):
                    v = Bc[:, :, a:a + c * w].rearrange("p h (c w) -> p h c w", w=w)
                    o = ke[:, :, a:a + c * w].rearrange("p h (c w) -> p h c w", w=w)
                    for h in range(GH):
                        ins = e.tensor_tensor(o[:, h], v[:, h, :, w - 1:w].broadcast_to([P, c, w]), v[:, h], ALU.subtract)
                    ins.then_inc(D_done, 1)
                e.wait_ge(exp_done, 1)
                f = lambda a: a.rearrange("p h n -> p (h n)")
                S_(e.tensor_tensor(f(qk[:, 0:GH]), f(qk[:, 0:GH]), f(expB), ALU.mult))
                e.tensor_copy(last, expB[:, :, GCH - 1:SEQ:GCH]).then_inc(kd_done, 1)
                e.tensor_copy(last_s, expB[:, :, SEQ + DEC_T - 1:N:DEC_T]).then_inc(kd_done, 1)
                e.wait_ge(exp_done, 2)
                e.tensor_tensor(f(ke), f(ke), f(qk[:, GH:]), ALU.mult).then_inc(kd_done, 1)
                e.wait_ge(exp_done, 3)
                e.tensor_tensor(f(qk[:, GH:]), f(qk[:, GH:]), f(Bc), ALU.mult).then_inc(kd_done, 1)
                e.wait_ge(kd_done, 4)
                for h in range(GH):
                    v = qsel[:, h].rearrange("p (b r) -> p b r", b=DEC_B)
                    for b in range(DEC_B):
                        ins = e.tensor_copy(v[:, b, b * DEC_T:(b + 1) * DEC_T], qk[:, h, SEQ + b * DEC_T:SEQ + (b + 1) * DEC_T])
                ins.then_inc(qsel_done, 2)
                for t, np_ in TILES:
                    e.wait_ge(ket_ps, t + 1)
                    e.tensor_copy(gtok[0:np_, t], ps[0:np_, t, :]).then_inc(ket_done, 1)

                def normalise(t, np_):
                    o = lambda h: ps[0:np_, 2 + h // 2, (h % 2) * GDV:(h % 2 + 1) * GDV]
                    e.wait_ge(o_ps, t + 1 if t < 4 else 8)
                    for h in range(GH):
                        ins = e.bn_stats(st[0:np_, h], o(h))
                    S_(ins)
                    for h in range(GH):
                        ins = e.bn_aggr(mv[0:np_, h], st[0:np_, h])
                    S_(ins)
                    e.tensor_scalar(rstd[0:np_], mv[0:np_, :, 1], LN_EPS, None, ALU.add).then_inc(ovar, 1)
                    e.wait_ge(ostd, t + 1)
                    S_(e.reciprocal(rstd[0:np_], rstd[0:np_]))
                    if t:
                        e.wait_ge(oT_ps, t)
                    for h in range(GH):
                        ins = e.tensor_scalar(onorm[0:np_, h * GDV:(h + 1) * GDV], o(h), mv[0:np_, h, 0:1], rstd[0:np_, h:h + 1],
                                              ALU.subtract, ALU.mult)
                    ins.then_inc(o_read, 1)
                    e.wait_ge(o_read, t + 1)
                    v = onorm[0:np_].rearrange("p (h v) -> p h v", h=GH)
                    S_(e.tensor_tensor(v, v, normg[0:np_].unsqueeze(1).broadcast_to([np_, GH, GDV]), ALU.mult))
                    e.wait_ge(vr_done, 20)
                    e.tensor_tensor(onorm[0:np_], onorm[0:np_], rtok[0:np_, t], ALU.mult).then_inc(on_done, 1)

                def mask_att(t, np_):
                    e.wait_ge(att_ps, t + 1)
                    if t >= 2:
                        e.wait_ge(o_ps, t - 1)
                    m = (K["chunk"] if t < 4 else K["chunk_s"][0:NS_TOK]).bitcast(I32)
                    for h in range(GH):
                        s = slice(h * P, h * P + np_)
                        ins = e.copy_predicated(attT[0:np_, t % 2, s], m, ps[0:np_, 5, s])
                    ins.then_inc(att_done, 1)

                for t in range(4):
                    mask_att(t, P)
                    for u in range(2):
                        n = 2 * t + u
                        e.wait_ge(ds_ps, n + 1)
                        if n >= 2:
                            e.wait_ge(o_ps, (n - 2) // 2 + 1)
                        for h in range(GH):
                            c = slice(h * GDV, (h + 1) * GDV)
                            dS = ps[:, 6 + h // 2, (h % 2) * GDV:(h % 2 + 1) * GDV]
                            if n:
                                ins = e.scalar_tensor_tensor(out=states[:, (n + 1) % 3, c], in0=states[:, n % 3, c],
                                                             scalar=last[:, h, n:n + 1], in1=dS, op0=ALU.mult, op1=ALU.add)
                            else:
                                ins = e.tensor_copy(states[:, 1, c], dS)
                        ins.then_inc(ds_done, 1)
                        e.wait_ge(ds_done, n + 1)
                    normalise(t, P)
                e.wait_ge(o_ps, 3)
                S_(e.memset(attT[:, 0], 0.0))
                mask_att(4, NS_TOK)
                for h in range(GH):
                    if h:
                        e.wait_ge(ds_ps, NCHUNK + 4 * h)
                    for b in range(DEC_B):
                        ins = e.tensor_scalar(kem[0:NS_TOK, b], gtok[0:NS_TOK, 4, h * P:(h + 1) * P], K["seqsel"][0:NS_TOK, b:b + 1],
                                              None, ALU.mult)
                    ins.then_inc(kem_done, 1)
                    e.wait_ge(S0_in[h % 2], 16 * (h // 2 + 1))
                    for q in range(4):
                        n = 4 * h + q
                        e.wait_ge(ds_ps, NCHUNK + n + 1)
                        for b in (2 * q, 2 * q + 1):
                            s = S0[:, h % 2, b * GDV:(b + 1) * GDV]
                            ins = e.scalar_tensor_tensor(out=s, in0=s, scalar=last_s[:, h, b:b + 1],
                                                         in1=ps[:, 6 + n % 2, (b % 2) * GDV:(b % 2 + 1) * GDV], op0=ALU.mult, op1=ALU.add)
                        ins.then_inc(ds_done, 1)
                normalise(4, NS_TOK)

            return sp, pe, act, dve, pool

        def stage_search(l):
            A = Arena(arena_buf, arena_w)
            slotT = A(3, N)
            qn = A(NT, 512)
            qT = A(2, 512)
            s1, s2 = A(NT, 512), A(4, NK)
            keyT = A(2, NK)
            V, If, sel = A(4, TOPK), A(4, TOPK), A(2, 2, TOPK)
            Iu, Ju, su = A(4, TOPK), A(2, TOPK), A(2, 2, TOPK)
            cand, cand2 = A(2, TOPK * TOPK), A(2, TOPK * TOPK)
            eq = A(2, 2 * TOPK * TOPK)
            E1, E2, G = A(NT, P), A(NT, P), A(NT, P)
            gd, gs = A(NT, P), A(NT, PH)
            st, mv, rstd = A(2, 6), A(2, 2), A(2)
            Iu, Ju, su = Iu.bitcast(U32), Ju.bitcast(U32), su.bitcast(U32)
            base = reserve(16)
            keys_in, slot_ps, slot_done = mark("keys_in", 16), mark("slot_ps", 1), mark("slotT_done", 2)
            qvar, qstd, qn_done, qT_ps, qT_done, sc_ps, sc_done, top_done = (mark(s, 4 * NT) for s in (
                "q_var", "q_std", "qn_done", "qT_ps", "qT_done", "score_ps", "score_done", "top_done"))
            diff_done, gexp_done, gates_done = (mark(s, NT) for s in ("gate_diff", "gate_exp", "gates_done"))

            def sp(e):
                for s in range(16):
                    ring.load(e, d["peer_wq"][l, s])

            def pool(e):
                e.dma_start(keyT, d["peer_keyT"][l]).then_inc(keys_in.sem, 16)

            def pe(e):
                e.wait_ge(*keys_in(16))
                for g in range(4):
                    for s in range(4):
                        slot = ring.take(e)
                        row_tiles(slot, 2 * s, e, hT, None, None, None, lambda t: t,
                                  before=(lambda t: e.wait_ge(*qn_done(5 * (g - 1) + t + 1))) if g else None)
                    for t, np_ in TILES:
                        n = 5 * g + t
                        e.wait_ge(*qn_done(n + 1))
                        if n:
                            e.wait_ge(*qT_done(n))
                        for j in range(4):
                            mm = transpose(e, ps[:, 5, j * P:j * P + np_], qn[0:np_, t, j * P:(j + 1) * P])
                        mm.then_inc(qT_ps.sem, 1)
                        e.wait_ge(*qT_done(n + 1))
                        if n >= 2:
                            e.wait_ge(*sc_done(n - 1))
                        for j in range(4):
                            mm = e.matmul(ps[0:np_, 6 + n % 2, j * P:(j + 1) * P], qT[:, n % 2, j * P:j * P + np_], keyT[:, j % 2],
                                          start=True, stop=True)
                        mm.then_inc(sc_ps.sem, 1)
                e.wait_ge(*gates_done(NT))
                for w, src in enumerate((E1, E2, G)):
                    for t, np_ in TILES:
                        o = ps[:, w, cols(t, np_)] if t < 4 else ps[:, 3, w * NS_TOK:(w + 1) * NS_TOK]
                        mm = transpose(e, o, src[0:np_, t])
                mm.then_inc(slot_ps.sem, 1)

            def act(e):
                for g in range(4):
                    for t, np_ in TILES:
                        n = 5 * g + t
                        e.wait_ge(*qvar(n + 1))
                        e.activation(rstd[0:np_], rstd[0:np_], ACT.Sqrt).then_inc(qstd.sem, 1)
                    for t, np_ in TILES:
                        n = 5 * g + t
                        e.wait_ge(*qT_ps(n + 1))
                        v = lambda a: a.rearrange("p (j n) -> p j n", j=4)[:, :, 0:np_]
                        e.activation(v(qT[:, n % 2]), v(ps[:, 5, :]), ACT.Copy).then_inc(qT_done.sem, 1)
                        e.wait_ge(*sc_ps(n + 1))
                        if g:
                            e.wait_ge(*top_done(n - 4))
                        e.activation(s1[0:np_, t], ps[0:np_, 6 + n % 2, :], ACT.Copy).then_inc(sc_done.sem, 1)
                for t, np_ in TILES:
                    e.wait_ge(*diff_done(t + 1))
                    e.activation(gd[0:np_, t], gd[0:np_, t], ACT.Exp).then_inc(gexp_done.sem, 1)

            def dve(e):
                S_ = dve_chain
                for g in range(4):
                    for t, np_ in TILES:
                        n = 5 * g + t
                        q = ps[0:np_, t, :]
                        e.wait_ge(used, base + 4 * (g + 1))
                        for h in range(2):
                            ins = e.bn_stats(st[0:np_, h], q[:, h * 256:(h + 1) * 256])
                        S_(ins)
                        for h in range(2):
                            ins = e.bn_aggr(mv[0:np_, h], st[0:np_, h])
                        S_(ins)
                        e.tensor_scalar(rstd[0:np_], mv[0:np_, :, 1], LN_EPS, None, ALU.add).then_inc(qvar.sem, 1)
                        e.wait_ge(*qstd(n + 1))
                        S_(e.reciprocal(rstd[0:np_], rstd[0:np_]))
                        if g:
                            e.wait_ge(*qT_ps(n - 4))
                        for h in range(2):
                            c = slice(h * 256, (h + 1) * 256)
                            ins = e.tensor_scalar(qn[0:np_, t, c], q[:, c], mv[0:np_, h, 0:1], rstd[0:np_, h:h + 1], ALU.subtract, ALU.mult)
                        ins.then_inc(qn_done.sem, 1)
                        e.wait_ge(*qn_done(n + 1))
                    for t, np_ in TILES:
                        n = 5 * g + t
                        r = slice(0, np_)
                        s = s1[r, t].rearrange("p (j n) -> p j n", j=4)
                        e.wait_ge(*sc_done(n + 1))
                        top16(e, S_, 4, lambda j: s[:, j], lambda j: s2[r, j], lambda j: V[r, j], lambda j: Iu[r, j])
                        Vv = V[r].rearrange("p (h w) k -> p h w k", w=2)
                        cv = cand[r].rearrange("p h (a b) -> p h a b", a=TOPK)
                        sh = [np_, TOPK, TOPK]
                        for h in range(2):
                            ins = e.tensor_tensor(cv[:, h], Vv[:, h, 0].unsqueeze(2).broadcast_to(sh), Vv[:, h, 1].unsqueeze(1).broadcast_to(sh), ALU.add)
                        S_(ins)
                        top16(e, S_, 2, lambda h: cand[r, h], lambda h: cand2[r, h], lambda h: G[r, t, (2 * g + h) * TOPK:(2 * g + h + 1) * TOPK],
                              lambda h: Ju[r, h])
                        e.tensor_scalar(su[r, 0], Ju[r], 4, None, ALU.logical_shift_right)
                        S_(e.tensor_scalar(su[r, 1], Ju[r], 15, None, ALU.bitwise_and))
                        e.tensor_copy(If[r], Iu[r])
                        S_(e.tensor_copy(sel[r], su[r]))
                        ev = eq[r].rearrange("p w (h a b) -> p w h a b", h=2, a=TOPK)
                        Iv = If[r].rearrange("p (h w) k -> p h w k", w=2)
                        it = K["iota"][r, 0:TOPK].unsqueeze(1).broadcast_to(sh)
                        for w in range(2):
                            for h in range(2):
                                ins = e.tensor_tensor(ev[:, w, h], it, sel[r, w, h].unsqueeze(2).broadcast_to(sh), ALU.is_equal)
                        S_(ins)
                        for w in range(2):
                            for h in range(2):
                                ins = e.tensor_tensor(ev[:, w, h], ev[:, w, h], Iv[:, h, w].unsqueeze(1).broadcast_to(sh), ALU.mult)
                        S_(ins)
                        for w, E_ in enumerate((E1, E2)):
                            ins = e.tensor_reduce(E_[r, t, 2 * g * TOPK:(2 * g + 2) * TOPK],
                                                  eq[r, w].rearrange("p (k b) -> p k b", b=TOPK), AX, ALU.add)
                        ins.then_inc(top_done.sem, 1)
                e.wait_ge(*top_done(20))
                for t, np_ in TILES:
                    v = G[0:np_, t].rearrange("p (h k) -> p h k", h=PH)
                    e.tensor_tensor(gd[0:np_, t].rearrange("p (h k) -> p h k", h=PH), v, v[:, :, 0:1].broadcast_to([np_, PH, TOPK]),
                                    ALU.subtract).then_inc(diff_done.sem, 1)
                for t, np_ in TILES:
                    v = gd[0:np_, t].rearrange("p (h k) -> p h k", h=PH)
                    e.wait_ge(*gexp_done(t + 1))
                    S_(e.tensor_reduce(gs[0:np_, t], v, AX, ALU.add))
                    S_(e.reciprocal(gs[0:np_, t], gs[0:np_, t]))
                    e.tensor_tensor(G[0:np_, t].rearrange("p (h k) -> p h k", h=PH), v, gs[0:np_, t].unsqueeze(2).broadcast_to([np_, PH, TOPK]),
                                    ALU.mult).then_inc(gates_done.sem, 1)
                e.wait_ge(*slot_ps(1))
                e.tensor_copy(slotT[:, :, 0:SEQ], ps[:, 0:3, :]).then_inc(slot_done.sem, 1)
                e.tensor_copy(slotT[:, :, SEQ:N], ps[:, 3, 0:3 * NS_TOK].rearrange("p (w n) -> p w n", w=3)).then_inc(slot_done.sem, 1)

            return sp, pe, act, dve, pool

        def top16(e, step, n, src, rest, val, idx):
            for j in range(n):
                ins = e.max(val(j)[:, 0:8], src(j))
            step(ins)
            for j in range(n):
                e.max_index(idx(j)[:, 0:8], val(j)[:, 0:8], src(j))
                ins = e.match_replace(rest(j), val(j)[:, 0:8], src(j), -3.0e38)
            step(ins)
            for j in range(n):
                ins = e.max(val(j)[:, 8:16], rest(j))
            step(ins)
            for j in range(n):
                ins = e.max_index(idx(j)[:, 8:16], val(j)[:, 8:16], rest(j))
            step(ins)

        def stage_gates(l):
            A = Arena(arena_buf, arena_w)
            slotT = A(3, N)
            cur = A(2, 3, 32)
            oh1, oh2 = A(2, 4, NK), A(2, 4, NK)
            gb = A(2, NK * 32)
            cur_done, oh1_done, oh2_done, oh_read, g_out = (mark(*s) for s in (
                ("slot_cur", NBLK), ("onehot1", 8 * NBLK), ("onehot2", 8 * NBLK), ("onehots_read", 8 * NBLK + 2), ("G_copied", 8 * NBLK + 8)))
            stored = [mark(f"G_stored{i}", 16 * ((NBLK + 1 - i) // 2 + 1)) for i in range(2)]

            def over_blocks(e, body):
                with e.Fori(0, NBLK // 2) as i:
                    for u in range(2):
                        body(i, u)
                body(NBLK // 2, 0)

            def pe(e):
                def body(i, u):
                    for q in range(8):
                        g = i * 16 + (8 * u + q)
                        e.wait_ge(*oh1_done(g + 1))
                        e.wait_ge(*oh2_done(g + 1))
                        e.wait_ge(*g_out(g + 1))
                        for k in range(4):
                            mm = e.matmul(ps[:, q, k * NK:(k + 1) * NK], oh1[:, q % 2, k], oh2[:, q % 2, k], start=True, stop=True)
                        mm.then_inc(oh_read.sem, 1)
                over_blocks(e, body)

            def pool(e):
                e.sem_inc(oh_read.sem, 2)

                def body(i, u):
                    e.wait_ge(*cur_done(i * 2 + (u + 1)))
                    for q in range(8):
                        g = i * 16 + (8 * u + q)
                        e.wait_ge(*oh_read(g + 1))
                        alone(e)
                        for k in range(4):
                            c = 4 * q + k
                            ins = e.tensor_scalar(oh1[:, q % 2, k], K["iota"], cur[:, u, 0, c:c + 1], None, ALU.is_equal)
                        ins.then_inc(oh1_done.sem, 1)
                over_blocks(e, body)

            def dve(e):
                e.wait_ge(*oh_read(2))

                def body(i, u):
                    b = i * 2 + u
                    e.tensor_copy(cur[:, u], slotT[:, :, bass.ds(b * 32, 32)]).then_inc(cur_done.sem, 1)
                    e.wait_ge(*cur_done(b + 1))
                    for q in range(8):
                        g = i * 16 + (8 * u + q)
                        e.wait_ge(*oh_read(g + 1))
                        for k in range(4):
                            c = 4 * q + k
                            ins = e.tensor_scalar(oh2[:, q % 2, k], K["iota"], cur[:, u, 1, c:c + 1], cur[:, u, 2, c:c + 1],
                                                  ALU.is_equal, ALU.mult)
                        ins.then_inc(oh2_done.sem, 1)
                over_blocks(e, body)

            def act(e):
                e.sem_inc(g_out.sem, 8)
                for u in range(2):
                    e.sem_inc(stored[u].sem, 16)

                def body(i, u):
                    e.wait_ge(*stored[u](i * 16 + 16))
                    for q in range(8):
                        g = i * 16 + (8 * u + q)
                        e.wait_ge(*oh_read(g + 3))
                        o = gb[:, u].rearrange("p (i n) -> p n i", n=32)[:, 4 * q:4 * q + 4]
                        e.activation(o, ps[:, q, :].rearrange("p (n i) -> p n i", n=4), ACT.Copy).then_inc(g_out.sem, 1)
                    e.wait_ge(*g_out(i * 16 + (8 * u + 16)))
                    e.dma_start(d["G"][bass.ds(i * 2 + u, 1)].rearrange("b p c -> (b p) c"), gb[:, u]).then_inc(stored[u].sem, 16)
                over_blocks(e, body)
                for u in range(2):
                    e.wait_ge(*stored[u](16 * (1 + (NBLK + 1 - u) // 2)))

            return lambda e: None, pe, act, dve, pool

        def stage_experts(l):
            A = Arena(arena_buf, arena_w)
            Y = A(KC, N)
            act_t, gel = A(TPG, N), A(2, N)
            gt = A(NBLK, TPG * 32)
            turns = NK // TPG
            base = reserve(turns * RING)
            g_in, h_read, a_done, y_ps, y_read, y_zero = (mark(*s) for s in (
                ("G_in", 16 * turns), ("H_read", TPG * turns + 2), ("A_done", TPG * turns + 2), ("Y_ps", (KC - 1) * turns),
                ("Y_read", KC * turns + 2), ("Y_zero", 1)))

            def sp(e):
                def src(i, j):
                    t = i * TPG + j % TPG
                    if j < TPG:
                        return d["peer_uT"][l, bass.ds(t, 1)].rearrange("a p c -> (a p) c")
                    return d["peer_v"][l][:, bass.ds(t * D, D)]
                ring.load_loop(e, src, 0, turns)

            def pe(e):
                with e.Fori(0, turns) as i:
                    for tt in range(TPG):
                        slot = ring.take(e, turn=i, j=tt)
                        e.wait_ge(*h_read(i * TPG + (tt + 1)))
                        for h in range(2):
                            for k in range(KC):
                                mm = e.matmul(ps[:, 2 * (tt % 2) + h, 0:HALF], slot[:, k * P:(k + 1) * P],
                                              hT[:, k, h * HALF:(h + 1) * HALF], start=(k == 0), stop=(k == KC - 1))
                        mm.then_inc(used, 1)
                    slots = [ring.take(e, turn=i, j=TPG + tt) for tt in range(TPG)]
                    e.wait_ge(*a_done(i * TPG + (TPG + 2)))
                    for m in range(KC):
                        e.wait_ge(*y_read(i * KC + (m + 1)))
                        for h in range(2):
                            for tt in range(TPG):
                                mm = e.matmul(ps[:, 4 + 2 * (m % 2) + h, 0:HALF], slots[tt][:, m * P:(m + 1) * P],
                                              act_t[:, tt, h * HALF:(h + 1) * HALF], start=(tt == 0), stop=(tt == TPG - 1))
                                if m == KC - 1 and h == 1:
                                    mm.then_inc(used, 1)
                        if m < KC - 1:
                            mm.then_inc(y_ps.sem, 1)
                ring.taken += turns * RING

            def act(e):
                e.sem_inc(h_read.sem, 2)
                with e.Fori(0, turns) as i:
                    for tt in range(TPG):
                        e.wait_ge(used, i * RING + (base + tt + 1))
                        e.wait_ge(*a_done(i * TPG + (tt + 1)))
                        e.activation(halves(gel[:, tt % 2]), pair(2 * (tt % 2)), ACT.Gelu).then_inc(h_read.sem, 1)

            def pool(e):
                with e.Fori(0, turns) as i:
                    e.wait_ge(*a_done(i * TPG + 2))
                    src = d["G"].rearrange("b p c -> p b c")[:, :, bass.ds(i * (TPG * 32), TPG * 32)]
                    e.dma_start(gt, src).then_inc(g_in.sem, 16)

            def dve(e):
                e.sem_inc(y_read.sem, 2)
                e.sem_inc(a_done.sem, 2)
                e.memset(Y.rearrange("p k n -> p (k n)"), 0.0).then_inc(y_zero.sem, 1)
                e.wait_ge(*y_zero(1))
                with e.Fori(0, turns) as i:
                    e.wait_ge(*g_in(i * 16 + 16))
                    for tt in range(TPG):
                        e.wait_ge(*h_read(i * TPG + (tt + 3)))
                        v = lambda a: a.rearrange("p (b n) -> p b n", n=32)
                        e.tensor_tensor(v(act_t[:, tt]), v(gel[:, tt % 2]), gt[:, :, tt * 32:(tt + 1) * 32], ALU.mult).then_inc(a_done.sem, 1)
                    for m in range(KC):
                        if m < KC - 1:
                            e.wait_ge(*y_ps(i * (KC - 1) + (m + 1)))
                        else:
                            e.wait_ge(used, i * RING + (base + RING))
                        e.tensor_tensor(halves(Y[:, m]), halves(Y[:, m]), pair(4 + 2 * (m % 2)), ALU.add).then_inc(y_read.sem, 1)

            return sp, pe, act, dve, pool

        def stage_latent():
            A = Arena(arena_buf, arena_w)
            cq = A(NT, QLORA)
            cqT = A(QC, N)
            gq, gkv = A(QLORA), A(KVL)
            qn, qlat, qr = A(N), A(2, 2, N), A(2, 2, N)
            junk = A(512)
            room = A.at = max(A.at, 2 * 5 * HPAGES * P + 17 * P + 20 * 32)
            ckv, kr = A(NT, KVL), A(NT, DR)
            ckvT, krT = A(2, N), A(N)
            wuk, wuv = A(MH, KVL), A(2, MH, P)
            prob, pT = A(2, 512), A(2, 512)
            ropef, ropet = A(2, N), A(2, NT, DR)
            qs, qrs = A(2, DEC_B, MH * DEC_T), A(DEC_B, MH * DEC_T)
            t1, t2 = A(N), A(N)
            ss, var, rstd = A(NT, 3), A(NT, 2), A(NT, 2)
            krr = A(NT, DR)
            small = A(8, 4)
            base = reserve(9)
            rows_in, ss_done, raw_done = sem("mla_rows_in"), sem("sumsq_done"), sem("raw_done")
            rvar, rstd_done, norm_done, lat_out = sem("rms_var"), sem("rms_std"), sem("latents_done"), sem("latents_out")
            cT_ps, cT_done = sem("latT_ps"), sem("latT_done")

            def sp(e):
                for s in range(9):
                    src = d["mla_win"][s]
                    ring.load(e, src if s < 8 else src[:, 0:KC * DR])

            def pool(e):
                e.dma_start(gq, d["mla_g_q"].broadcast_to([P, QLORA])).then_inc(rows_in, 16)
                e.dma_start(gkv, d["mla_g_kv"].broadcast_to([P, KVL])).then_inc(rows_in, 16)
                e.dma_start(wuk, d["wukT"]).then_inc(rows_in, 16)
                e.dma_start(wuv, d["wuv"]).then_inc(rows_in, 16)
                e.dma_start(ropef, d["rope_feat"]).then_inc(rows_in, 16)
                e.dma_start(ropet, d["rope_tok"]).then_inc(rows_in, 16)
                for t, np_ in TILES:
                    e.wait_ge(norm_done, t + 1)
                    r = slice(t * P, t * P + np_)
                    e.dma_start(d["o_ckv"][r], ckv[0:np_, t]).then_inc(lat_out, 16)
                    e.dma_start(d["o_kr"][r], krr[0:np_, t]).then_inc(lat_out, 16)
                e.wait_ge(lat_out, 160)

            def pe(e):
                for g in range(2):
                    for s in range(4):
                        slot = ring.take(e)
                        row_tiles(slot, 2 * s, e, hT, None, None, None, lambda t: (5 * g + t) % 8,
                                  before=(lambda t: e.wait_ge(raw_done, t - 2) if t >= 3 else None) if g else None)
                slot = ring.take(e)
                e.wait_ge(raw_done, 10)
                row_tiles(slot, 0, e, hT, None, None, None, lambda t: t, width=DR)
                for t, np_ in TILES:
                    e.wait_ge(norm_done, t + 1)
                    if t:
                        e.wait_ge(cT_done, t)
                    for k in range(QC):
                        transpose(e, ps[:, 5 + k // 4, (k % 4) * P:(k % 4) * P + np_], cq[0:np_, t, k * P:(k + 1) * P])
                    for k in range(2):
                        transpose(e, ps[:, 6, (2 + k) * P:(2 + k) * P + np_], ckv[0:np_, t, k * P:(k + 1) * P])
                    transpose(e, ps[0:DR, 7, 0:np_], krr[0:np_, t]).then_inc(cT_ps, 1)

            def act(e):
                for g in range(2):
                    for t, np_ in TILES:
                        e.wait_ge(used, base + 4 * (g + 1))
                        b = (5 * g + t) % 8
                        if g or t:
                            e.wait_ge(ss_done, 5 * g + (t if g == 0 else 2 * t))
                        if g == 0:
                            e.activation(junk[0:np_], ps[0:np_, b, :], ACT.Square, accum_out=ss[0:np_, t, 0:1]).then_inc(ss_done, 1)
                        else:
                            for w in range(2):
                                e.wait_ge(ss_done, 5 + 2 * t + w)
                                e.activation(junk[0:np_, 0:256], ps[0:np_, b, w * 256:(w + 1) * 256], ACT.Square,
                                             accum_out=ss[0:np_, t, 1 + w:2 + w]).then_inc(ss_done, 1)
                e.wait_ge(rvar, 1)
                e.activation(rstd, var, ACT.Sqrt).then_inc(rstd_done, 1)
                for t, np_ in TILES:
                    e.wait_ge(cT_ps, t + 1)
                    v = ps[:, 5:7, :].rearrange("p b (k n) -> p (b k) n", k=4)
                    e.activation(cqT[:, :, cols(t, np_)], v[:, 0:QC, 0:np_], ACT.Copy)
                    e.activation(ckvT[:, :, cols(t, np_)], v[:, QC:QC + 2, 0:np_], ACT.Copy)
                    e.activation(krT[0:DR, cols(t, np_)], ps[0:DR, 7, 0:np_], ACT.Copy).then_inc(cT_done, 1)

            def dve(e):
                S_ = dve_chain
                S_(e.memset(var, 1.0))
                e.wait_ge(rows_in, 96)
                for g in range(2):
                    for t, np_ in TILES:
                        e.wait_ge(ss_done, t + 1 if g == 0 else 5 + 2 * (t + 1))
                        b = (5 * g + t) % 8
                        if g == 0:
                            e.tensor_copy(cq[0:np_, t, 0:512], ps[0:np_, b, :]).then_inc(raw_done, 1)
                        else:
                            S_(e.tensor_copy(cq[0:np_, t, 512:768], ps[0:np_, b, 0:256]))
                            e.tensor_copy(ckv[0:np_, t], ps[0:np_, b, 256:512]).then_inc(raw_done, 1)
                            S_(e.tensor_tensor(ss[0:np_, t, 0:1], ss[0:np_, t, 0:1], ss[0:np_, t, 1:2], ALU.add))
                            e.tensor_scalar(var[0:np_, t, 0:1], ss[0:np_, t, 0:1], 1.0 / QLORA, RMS_EPS, ALU.mult, ALU.add)
                            S_(e.tensor_scalar(var[0:np_, t, 1:2], ss[0:np_, t, 2:3], 1.0 / KVL, RMS_EPS, ALU.mult, ALU.add))
                e.wait_ge(raw_done, 10)
                e.sem_inc(rvar, 1)
                e.wait_ge(used, base + 9)
                for t, np_ in TILES:
                    S_(e.tensor_copy(kr[0:np_, t], ps[0:np_, t, 0:DR]))
                e.wait_ge(rstd_done, 1)
                S_(e.reciprocal(rstd, rstd))
                for t, np_ in TILES:
                    r = slice(0, np_)
                    S_(e.scalar_tensor_tensor(out=cq[r, t], in0=cq[r, t], scalar=rstd[r, t, 0:1], in1=gq[r], op0=ALU.mult, op1=ALU.mult))
                    S_(e.scalar_tensor_tensor(out=ckv[r, t], in0=ckv[r, t], scalar=rstd[r, t, 1:2], in1=gkv[r], op0=ALU.mult, op1=ALU.mult))
                    hf = DR // 2
                    e.tensor_tensor(t2[r, 0:hf], kr[r, t, hf:DR], ropet[r, 1, t, 0:hf], ALU.mult)
                    e.tensor_tensor(t2[r, hf:DR], kr[r, t, 0:hf], ropet[r, 1, t, hf:DR], ALU.mult)
                    S_(e.tensor_tensor(t1[r, 0:DR], kr[r, t], ropet[r, 0, t], ALU.mult))
                    e.tensor_tensor(krr[r, t], t1[r, 0:DR], t2[r, 0:DR], ALU.add).then_inc(norm_done, 1)

            stages.append((sp, pe, act, dve, pool))

            hbase = reserve(MH + MH // 2)
            hslot = lambda h: hbase + h + h // 2 + 1
            qn_done, ql_ps, ql_done, rp_done = sem("qnope_done"), sem("qlat_ps"), sem("qlat_done"), sem("qrope_done")
            sc_ps, nmax_done, p_done, pn_done = sem("att_scores"), sem("att_nmax"), sem("att_exp"), sem("att_prob")
            pT_ps, pT_done, ol_ps, ol_done, uv_ps, uv_done = (sem(s) for s in (
                "att_pT_ps", "att_pT", "olat_ps", "olat_done", "uv_ps", "uv_done"))
            olat = A(2, 2, SEQ)

            def sp2(e):
                for h in range(MH):
                    if h % 2 == 0:
                        ring.load(e, d["wuq_rope"][h // 2])
                    ring.load(e, d["wuq_nope"][h])

            def pe2(e):
                def project(slot, b):
                    for h2 in range(2):
                        for k in range(QC):
                            mm = e.matmul(ps[:, b + h2, 0:HALF], slot[:, k * P:(k + 1) * P], cqT[:, k, h2 * HALF:(h2 + 1) * HALF],
                                          start=(k == 0), stop=(k == QC - 1))
                    mm.then_inc(used, 1)

                def finish(n):
                    h, i = divmod(n, 4)
                    e.wait_ge(pn_done, n + 1)
                    if n:
                        e.wait_ge(pT_done, n)
                    for j in range(i + 1):
                        mm = transpose(e, ps[:, 2, j * P:(j + 1) * P], prob[:, n % 2, j * P:(j + 1) * P])
                    mm.then_inc(pT_ps, 1)
                    e.wait_ge(pT_done, n + 1)
                    if n:
                        e.wait_ge(ol_done, n)
                    for c in range(2):
                        for j in range(i + 1):
                            mm = e.matmul(ps[:, 3, c * P:(c + 1) * P], ckv[:, j, c * P:(c + 1) * P], pT[:, n % 2, j * P:(j + 1) * P],
                                          start=(j == 0), stop=(j == i))
                    mm.then_inc(ol_ps, 1)

                def values(h):
                    e.wait_ge(ol_done, 4 * (h + 1))
                    if h:
                        e.wait_ge(uv_done, h)
                    for c in range(2):
                        mm = e.matmul(ps[:, 4, :], wuv[:, c, h], olat[:, h % 2, c], start=(c == 0), stop=(c == 1))
                    mm.then_inc(uv_ps, 1)

                for h in range(MH):
                    if h % 2 == 0:
                        slot = ring.take(e)
                        if h:
                            e.wait_ge(ql_done, 2 * h)
                        project(slot, 5)
                        e.wait_ge(rp_done, h // 2 + 1)
                    slot = ring.take(e)
                    if h % 2:
                        e.wait_ge(ql_done, 2 * h)
                    project(slot, 5)
                    e.wait_ge(qn_done, h + 1)
                    for c in range(2):
                        if c:
                            e.wait_ge(ql_done, 2 * h + 1)
                        for h2 in range(2):
                            mm = e.matmul(ps[:, 5 + h2, 0:HALF], wuk[:, h, c * P:(c + 1) * P], qn[:, h2 * HALF:(h2 + 1) * HALF], start=True, stop=True)
                        mm.then_inc(ql_ps, 1)
                    e.wait_ge(ql_done, 2 * h + 2)
                    for i in range(4):
                        n = 4 * h + i
                        w = (i + 1) * P
                        if n >= 2:
                            e.wait_ge(p_done, n - 1)
                        o = ps[:, n % 2, 0:w]
                        for c in range(2):
                            e.matmul(o, qlat[:, h % 2, c, cols(i, P)], ckvT[:, c, 0:w], start=(c == 0), stop=False)
                        e.matmul(o, qrv(h)[:, cols(i, P)], krT[0:DR, 0:w],
                                 start=False, stop=True).then_inc(sc_ps, 1)
                        if n:
                            finish(n - 1)
                    if h:
                        values(h - 1)
                finish(4 * MH - 1)
                values(MH - 1)

            def qrv(h):
                return qr[0:DR, h % 2, (h // 2) % 2]

            def act2(e):
                for h in range(MH):
                    e.wait_ge(used, hslot(h) + 1)
                    if h:
                        e.wait_ge(ql_ps, 2 * h)
                    e.activation(halves(qn), pair(5), ACT.Copy).then_inc(qn_done, 1)
                    for c in range(2):
                        e.wait_ge(ql_ps, 2 * h + c + 1)
                        if h >= 2 and c == 0:
                            e.wait_ge(sc_ps, 4 * (h - 1))
                        e.activation(halves(qlat[:, h % 2, c]), pair(5), ACT.Copy).then_inc(ql_done, 1)
                    for i in range(4):
                        n = 4 * h + i
                        w = (i + 1) * P
                        e.wait_ge(nmax_done, n + 1)
                        e.activation(prob[:, n % 2, 0:w], ps[:, n % 2, 0:w], ACT.Exp, bias=small[:, 1 + n % 2, 0:1], scale=MSCALE,
                                     accum_out=small[:, 3 + n % 2, 0:1]).then_inc(p_done, 1)
                        m = n - 1
                        if m >= 0:
                            copy_pT(e, m)
                copy_pT(e, 4 * MH - 1)

            def copy_pT(e, m):
                w = (m % 4 + 1) * P
                e.wait_ge(pT_ps, m + 1)
                e.activation(pT[:, m % 2, 0:w], ps[:, 2, 0:w], ACT.Copy).then_inc(pT_done, 1)

            def dve2(e):
                S_ = dve_chain

                def rope_pair(hp):
                    e.wait_ge(used, hslot(2 * hp))
                    if hp:
                        e.wait_ge(ql_done, 4 * hp)
                    if hp >= 2:
                        e.wait_ge(sc_ps, 8 * (hp - 1))
                    src = pair(5)
                    for q in range(4):
                        a, b = slice(32 * q, 32 * q + 32), slice(32 * (q ^ 1), 32 * (q ^ 1) + 32)
                        ins = e.tensor_tensor(halves(t2[a]), src[b], halves(ropef[b, 1]), ALU.mult)
                    S_(ins)
                    S_(e.tensor_tensor(halves(t1), src, halves(ropef[:, 0]), ALU.mult))
                    for u in range(2):
                        r = slice(DR * u, DR * (u + 1))
                        ins = e.tensor_tensor(qr[0:DR, u, hp % 2], t1[r], t2[r], ALU.add)
                        if u == 0:
                            S_(ins)
                    ins.then_inc(rp_done, 1)
                    e.wait_ge(rp_done, hp + 1)

                def after(m):
                    e.wait_ge(ol_ps, m + 1)
                    if m % 4 == 0 and m >= 8:
                        e.wait_ge(uv_ps, m // 4 - 1)
                    v = ps[:, 3, 0:2 * P].rearrange("p (c n) -> p c n", c=2)
                    e.tensor_copy(olat[:, (m // 4) % 2, :, cols(m % 4, P)], v).then_inc(ol_done, 1)

                def out_values(h):
                    e.wait_ge(uv_ps, h + 1)
                    e.tensor_copy(hT[:, h, 0:SEQ], ps[:, 4, :]).then_inc(uv_done, 1)

                for h in range(MH):
                    if h % 2 == 0:
                        rope_pair(h // 2)
                    e.wait_ge(ql_done, 2 * h + 2)
                    hs = slice(h * DEC_T, (h + 1) * DEC_T)
                    e.tensor_copy(qs[:, :, :, hs], qlat[:, h % 2, :, SEQ:N].rearrange("p c (s t) -> p c s t", t=DEC_T))
                    S_(e.tensor_copy(qrs[0:DR, :, hs], qrv(h)[:, SEQ:N].rearrange("p (s t) -> p s t", t=DEC_T)))
                    for i in range(4):
                        n = 4 * h + i
                        w = (i + 1) * P
                        s = ps[:, n % 2]
                        e.wait_ge(sc_ps, n + 1)
                        S_(e.tensor_tensor(s[:, w - P:w], s[:, w - P:w], K["causal"], ALU.add))
                        S_(e.tensor_reduce(small[:, 0, 0:1], s[:, 0:w], AX, ALU.max))
                        if n >= 2:
                            e.wait_ge(p_done, n - 1)
                        e.tensor_scalar(small[:, 1 + n % 2, 0:1], small[:, 0, 0:1], -MSCALE, None, ALU.mult).then_inc(nmax_done, 1)
                        if n:
                            after(n - 1)
                        e.wait_ge(p_done, n + 1)
                        S_(e.reciprocal(small[:, 5 + n % 2, 0:1], small[:, 3 + n % 2, 0:1]))
                        e.tensor_scalar(prob[:, n % 2, 0:w], prob[:, n % 2, 0:w], small[:, 5 + n % 2, 0:1], None, ALU.mult).then_inc(pn_done, 1)
                    if h:
                        out_values(h - 1)
                after(4 * MH - 1)
                out_values(MH - 1)

            stages.append((sp2, pe2, act2, dve2, lambda e: None))

            B = Arena(arena_buf, arena_w)
            kc, krp, vp = B(2, 2, HPAGES * P), B(2, HPAGES * P), B(2, HPAGES, KVL)
            pr = B(17 * P)
            prT = B(16, 32)
            prnT = B(32)
            qcur = B(3, 32)
            assert B.at <= room
            olS = A(2, MH, NS_TOK)
            new_c, cur_c, cur_new = A(DEC_B, KVL), A(KVL), A(3, DEC_T)
            table = A(P).bitcast(I32)
            table_in, new_in = sem("page_table_in"), sem("new_latents_in")
            page_in = [sem("pages_in0"), sem("pages_in1")]
            cur_done, s_ps, s_nmax, s_exp, s_prob, s_pT_ps, s_pT, s_ol, s_ol_done = (sem("smp_" + s) for s in (
                "cur", "scores", "nmax", "exp", "prob", "pT_ps", "pT", "olat_ps", "olat"))
            u_ps, u_done = sem("smp_uv_ps"), sem("smp_uv")

            def sp3(e):
                e.wait_ge(stage_over, 4 * page_stage[0])
                e.dma_start(table[0:1], d["page_table"]).then_inc(table_in, 16)
                e.wait_ge(table_in, 16)
                with e.register("page") as reg:
                    with e.Fori(0, DEC_B) as b:
                        for hf in range(2):
                            e.wait_ge(s_ol_done, b + 1)
                            for q in range(HPAGES):
                                e.reg_load(reg, table[0:1, bass.ds(b * NPAGE + (hf * HPAGES + q), 1)])
                                pg = e.snap(reg, min_val=0, max_val=d["ckvT"].shape[0] - 1)
                                c = slice(q * P, (q + 1) * P)
                                one = lambda a: a[bass.ds(pg, 1)]
                                e.dma_start(kc[:, hf, :, c], one(d["ckvT"]).rearrange("a p c n -> (a p) c n")).then_inc(page_in[hf], 16)
                                e.dma_start(krp[0:DR, hf, c], one(d["krT"]).rearrange("a p n -> (a p) n")).then_inc(page_in[hf], 16)
                                e.dma_start(vp[:, hf, q], one(d["ckv_pool"]).rearrange("a p n -> (a p) n")).then_inc(page_in[hf], 16)

            def pool3(e):
                e.dma_start(new_c[0:DEC_T], d["o_ckv"][SEQ:N].rearrange("(s t) c -> t s c", t=DEC_T)).then_inc(new_in, 16)

            def pe3(e):
                with e.Fori(0, DEC_B) as b:
                    e.wait_ge(cur_done, b + 1)
                    e.wait_ge(s_exp, b + 1)
                    for hf in range(2):
                        e.wait_ge(page_in[hf], (b + 1) * (16 * 3 * HPAGES))
                        for w in range(2):
                            o = ps[0:32, 2 * hf + w, :]
                            c = slice(w * 512, (w + 1) * 512)
                            for k in range(2):
                                e.matmul(o, qcur[:, k], kc[:, hf, k, c], start=(k == 0), stop=False)
                            e.matmul(o, qcur[0:DR, 2], krp[0:DR, hf, c], start=False, stop=True)
                    o = ps[0:32, 4, 0:DEC_T]
                    for k in range(2):
                        e.matmul(o, qcur[:, k], cur_new[:, k], start=(k == 0), stop=False)
                    e.matmul(o, qcur[0:DR, 2], cur_new[0:DR, 2], start=False, stop=True).then_inc(s_ps, 1)
                    e.wait_ge(s_prob, b + 1)
                    alone(e)
                    for q in range(NPAGE):
                        transpose(e, ps[:, 5, q * 32:(q + 1) * 32], pr[0:32, q * P:(q + 1) * P])
                    transpose(e, ps[0:DEC_T, 6, 0:32], pr[0:32, PAST:PAST + DEC_T]).then_inc(s_pT_ps, 1)
                    e.wait_ge(s_pT, b + 1)
                    for c in range(2):
                        o = ps[:, 7, c * 32:(c + 1) * 32]
                        for q in range(NPAGE):
                            e.matmul(o, vp[:, q // HPAGES, q % HPAGES, c * P:(c + 1) * P], prT[:, q], start=(q == 0), stop=False)
                        mm = e.matmul(o, cur_c[0:DEC_T, c * P:(c + 1) * P], prnT[0:DEC_T], start=False, stop=True)
                    mm.then_inc(s_ol, 1)
                e.wait_ge(s_ol_done, DEC_B + 1)
                for h in range(MH):
                    for c in range(2):
                        mm = e.matmul(ps[:, 0, h * 32:(h + 1) * 32], wuv[:, c, h], olS[:, c, h], start=(c == 0), stop=(c == 1))
                mm.then_inc(u_ps, 1)

            def act3(e):
                e.sem_inc(s_exp, 1)
                with e.Fori(0, DEC_B) as b:
                    e.wait_ge(s_nmax, b + 1)
                    e.activation(pr[0:32, 0:PAST], ps[0:32, 0:4, :].rearrange("p b n -> p (b n)"), ACT.Exp, bias=small[0:32, 1, 0:1],
                                 scale=MSCALE, accum_out=small[0:32, 2, 0:1])
                    e.activation(pr[0:32, PAST:PAST + DEC_T], small[0:32, 0, 0:DEC_T], ACT.Exp, bias=small[0:32, 1, 0:1], scale=MSCALE,
                                 accum_out=small[0:32, 3, 0:1]).then_inc(s_exp, 1)

            def dve3(e):
                S_ = sem("sample_step")
                e.sem_inc(s_ol_done, 1)
                e.wait_ge(new_in, 16)
                per = 6
                with e.Fori(0, DEC_B) as b:
                    at = lambda n: b * per + n
                    one = bass.ds(b, 1)
                    e.tensor_copy(qcur[:, 0:2], qs[:, :, one].rearrange("p c s n -> p c (s n)"))
                    e.tensor_copy(qcur[0:DR, 2], qrs[0:DR, one].rearrange("p s n -> p (s n)"))
                    own = bass.ds(b * DEC_T + SEQ, DEC_T)
                    e.tensor_copy(cur_new[:, 0:2], ckvT[:, :, own])
                    e.tensor_copy(cur_new[0:DR, 2], krT[0:DR, own])
                    e.tensor_copy(cur_c[0:DEC_T], new_c[0:DEC_T, one].rearrange("p s c -> p (s c)")).then_inc(cur_done, 1)
                    e.wait_ge(s_ps, b + 1)
                    e.tensor_reduce(small[0:32, 4, 0:1], ps[0:32, 0:4, :].rearrange("p b n -> p (b n)"), AX, ALU.max)
                    e.tensor_tensor(small[0:32, 0, 0:DEC_T], ps[0:32, 4, 0:DEC_T], K["causal_s"][0:32], ALU.add).then_inc(S_, 1)
                    e.wait_ge(S_, at(1))
                    e.tensor_reduce(small[0:32, 4, 1:2], small[0:32, 0, 0:DEC_T], AX, ALU.max).then_inc(S_, 1)
                    e.wait_ge(S_, at(2))
                    e.tensor_reduce(small[0:32, 4, 2:3], small[0:32, 4, 0:2], AX, ALU.max).then_inc(S_, 1)
                    e.wait_ge(S_, at(3))
                    e.tensor_scalar(small[0:32, 1, 0:1], small[0:32, 4, 2:3], -MSCALE, None, ALU.mult).then_inc(s_nmax, 1)
                    e.wait_ge(s_exp, b + 2)
                    e.tensor_tensor(small[0:32, 5, 0:1], small[0:32, 2, 0:1], small[0:32, 3, 0:1], ALU.add).then_inc(S_, 1)
                    e.wait_ge(S_, at(4))
                    e.reciprocal(small[0:32, 6, 0:1], small[0:32, 5, 0:1]).then_inc(S_, 1)
                    e.wait_ge(S_, at(5))
                    e.tensor_scalar(pr[0:32, 0:PAST + DEC_T], pr[0:32, 0:PAST + DEC_T], small[0:32, 6, 0:1], None, ALU.mult).then_inc(s_prob, 1)
                    e.wait_ge(s_pT_ps, b + 1)
                    e.tensor_copy(prT.rearrange("p q n -> p (q n)"), ps[:, 5, :]).then_inc(S_, 1)
                    e.tensor_copy(prnT[0:DEC_T], ps[0:DEC_T, 6, 0:32]).then_inc(s_pT, 1)
                    e.wait_ge(s_ol, b + 1)
                    for c in range(2):
                        o = olS[:, c, :, bass.ds(b * DEC_T, DEC_T)]
                        ins = e.tensor_copy(o, ps[:, 7, c * 32:(c + 1) * 32].rearrange("p (h t) -> p h t", t=DEC_T))
                    ins.then_inc(s_ol_done, 1)
                e.wait_ge(u_ps, 1)
                e.tensor_copy(hT[:, :, SEQ:N], ps[:, 0, 0:MH * 32].rearrange("p (h n) -> p h n", h=MH)).then_inc(u_done, 1)

            page_stage = [len(stages)]
            stages.append((sp3, pe3, act3, dve3, pool3))

        stages.append(stage_ada())
        stages.append(stage_modulate(0, 0))
        stages.append(stage_gla())
        stages.append(stage_close(0, 0, w_o="gla_wo"))

        def peer(l):
            stages.append(stage_modulate(l, 1))
            stages.append(stage_search(l))
            stages.append(stage_gates(l))
            stages.append(stage_experts(l))
            stages.append(stage_close(l, 1, yT=Arena(arena_buf, arena_w)(KC, N)))

        peer(0)
        stages.append(stage_modulate(1, 0))
        stage_latent()
        stages.append(stage_close(1, 0, w_o="mla_wo"))
        peer(1)
        y_out = sem("y_out")

        def store(e):
            for t, np_ in TILES:
                e.dma_start(d["o_y"][t * P:t * P + np_], x[0:np_, t]).then_inc(y_out, 16)
            e.wait_ge(y_out, 16 * NT)

        stages.append((lambda e: None, lambda e: None, store, lambda e: None, lambda e: None))

        def run(eng, which):
            for n, s in enumerate(stages):
                if n and which:
                    eng.wait_ge(stage_over, 4 * n)
                s[which](eng)
                if which:
                    eng.drain().then_inc(stage_over, 1)

        block = ctx.enter_context(nc.Block())

        @block.sync
        def _(sp):
            run(sp, 0)

        @block.tensor
        def _(pe):
            run(pe, 1)

        @block.scalar
        def _(act):
            run(act, 2)

        @block.vector
        def _(dve):
            run(dve, 3)

        @block.gpsimd
        def _(pool):
            run(pool, 4)


def kernel(x_prompt, x_sample, c_prompt, c_sample, cache_ckv, cache_krope, state_gla, page_table, ada_w, ada_b,
           ln_g, ln_b, gla_w_in, gla_w_g2, gla_b_g, gla_norm_g, gla_w_o, mla_w_in, mla_g_q, mla_g_kv, mla_w_uq,
           mla_w_uk, mla_w_uv, mla_w_o, peer_w_q, peer_k1, peer_k2, peer_u, peer_v):
    import concourse.bacc as bacc
    from concourse.bass_utils import run_bass_kernel_spmd

    a = {k: np.asarray(v) for k, v in dict(locals()).items() if k not in ("bacc", "run_bass_kernel_spmd")}
    con, rope_tok, rope_feat = constants()
    cat = np.concatenate

    def rows(w):
        return w.reshape(4, 2, P, -1, 512).transpose(3, 0, 2, 1, 4).reshape(-1, P, SLOT)

    def blocks(w):
        r = w.shape[0] // P
        return w.reshape(r, P, -1, P).transpose(2, 1, 0, 3).reshape(-1, P, r * P)

    hk, hv = GH * GDK, GH * GDV
    gw, mw = a["gla_w_in"][0], a["mla_w_in"][0]
    uq = a["mla_w_uq"][0].reshape(QLORA, MH, DN + DR)
    ins = {
        "con": con, "rope_tok": rope_tok, "rope_feat": rope_feat,
        "cT": cat([a["c_prompt"], a["c_sample"]]).T.reshape(KC, P, NSEQ).transpose(1, 0, 2).reshape(P, -1),
        "ada_w": a["ada_w"].reshape(2, KC, P, 6, D).transpose(0, 3, 1, 2, 4).reshape(-1, P, D),
        "ada_b": a["ada_b"].reshape(1, -1),
        "x": cat([a["x_prompt"].reshape(SEQ, D), a["x_sample"].reshape(NS_TOK, D)]),
        "ln_g": a["ln_g"].reshape(4, D), "ln_b": a["ln_b"].reshape(4, D),
        "gla_w": cat([blocks(gw[:, :2 * hk]), rows(gw[:, 2 * hk:2 * hk + 2 * hv])]),
        "gla_wgl": gw[:, 2 * hk + 2 * hv:].reshape(KC, P, 16).transpose(1, 0, 2).reshape(P, -1),
        "gla_wg2": cat([a["gla_w_g2"][0], a["gla_b_g"]]),
        "gla_norm_g": a["gla_norm_g"],
        "gla_wo": rows(a["gla_w_o"][0]),
        "state_gla": a["state_gla"][0],
        "mla_win": cat([rows(mw[:, :1024]), np.pad(mw[:, 1024:].reshape(KC, P, DR).transpose(1, 0, 2).reshape(1, P, -1),
                                                   ((0, 0), (0, 0), (0, SLOT - KC * DR)))]),
        "mla_g_q": a["mla_g_q"], "mla_g_kv": a["mla_g_kv"],
        "wuq_nope": blocks(uq[:, :, :DN].reshape(QLORA, -1)), "wuq_rope": blocks(uq[:, :, DN:].reshape(QLORA, -1)),
        "wukT": a["mla_w_uk"][0].transpose(2, 1, 0).reshape(P, -1),
        "wuv": a["mla_w_uv"][0].reshape(2, P, MH * P).transpose(1, 0, 2).reshape(P, -1),
        "mla_wo": rows(a["mla_w_o"][0]),
        "ckvT": a["cache_ckv"][0].reshape(-1, PAGE, 2, P).transpose(0, 3, 2, 1),
        "krT": a["cache_krope"][0].transpose(0, 2, 1),
        "ckv_pool": a["cache_ckv"][0],
        "page_table": a["page_table"].reshape(1, -1),
        "peer_wq": np.stack([rows(a["peer_w_q"][l]) for l in range(2)]),
        "peer_keyT": np.stack([np.stack([a[k][l].T for k in ("peer_k1", "peer_k2")], 1).reshape(P, -1) for l in range(2)]),
        "peer_uT": a["peer_u"].reshape(2, NK, NK, KC, P).transpose(0, 2, 4, 3, 1).reshape(2, NK, P, D),
        "peer_v": a["peer_v"].reshape(2, NK, NK * D),
    }
    outs = {"o_y": (N, D), "o_gla_p": (GH, GDK, GDV), "o_gla_s": (DEC_B, GH, GDK, GDV), "o_ckv": (N, KVL), "o_kr": (N, DR)}
    nc = bacc.Bacc("TRN2", target_bir_lowering=False, num_devices=1)
    arrays, d = {}, {}
    for name, v in ins.items():
        v = np.ascontiguousarray(v)
        arrays["in_" + name] = v
        d[name] = nc.dram_tensor("in_" + name, v.shape, mybir.dt.from_np(v.dtype), kind="ExternalInput").ap()
    for name, shape in outs.items():
        d[name] = nc.dram_tensor(name, shape, F32, kind="ExternalOutput").ap()
    d["mod"] = nc.dram_tensor("mod_rows", (NSEQ, 12 * D), F32, kind="Internal").ap()
    d["G"] = nc.dram_tensor("gates_dense", (NBLK, P, NK * 32), F32, kind="Internal").ap()
    for name, k in (("cT", KC), ("gla_wgl", KC)):
        d[name] = d[name].rearrange("p (k n) -> p k n", k=k)
    d["peer_keyT"] = d["peer_keyT"].rearrange("l p (w n) -> l p w n", w=2)
    d["wukT"] = d["wukT"].rearrange("p (h c) -> p h c", h=MH)
    d["wuv"] = d["wuv"].rearrange("p (c h v) -> p c h v", c=2, h=MH)
    d["rope_feat"] = d["rope_feat"].rearrange("p (w n) -> p w n", w=2)
    d["rope_tok"] = d["rope_tok"].rearrange("p (w t n) -> p w t n", w=2, t=NT)
    build(nc, d)
    r = run_bass_kernel_spmd(nc, [arrays], core_ids=[0]).results[0]
    y, ckv, kr = r["o_y"], r["o_ckv"], r["o_kr"]
    return (y[:SEQ].reshape(1, SEQ, D), y[SEQ:].reshape(DEC_B, DEC_T, D),
            r["o_gla_p"].reshape(1, 1, GH, GDK, GDV), r["o_gla_s"].reshape(1, DEC_B, GH, GDK, GDV),
            ckv[:SEQ].reshape(1, 1, SEQ, KVL), kr[:SEQ].reshape(1, 1, SEQ, DR),
            ckv[SEQ:].reshape(1, DEC_B, DEC_T, KVL), kr[SEQ:].reshape(1, DEC_B, DEC_T, DR))
```

```python
import numpy as np
import concourse.bass as bass
from concourse import mybir
from contextlib import ExitStack

F32 = mybir.dt.float32
F32R = mybir.dt.float32r
I32 = mybir.dt.int32
U32 = mybir.dt.uint32
ALU = mybir.AluOpType
ACT = mybir.ActivationFunctionType
AX = mybir.AxisListType.X

P = 128
D = 1024
KC = D // P
SEQ, DEC_B, DEC_T, PAST, PAGE = 512, 8, 4, 2048, 128
NS_TOK = DEC_B * DEC_T
N = SEQ + NS_TOK
HALF = N // 2
TILES = [(i, P) for i in range(SEQ // P)] + [(SEQ // P, NS_TOK)]
NT = len(TILES)
NSEQ = 1 + DEC_B
ALPHA = 4.0 ** 0.25
LN_EPS, RMS_EPS, NEG = 1e-5, 1e-6, -1e30
GH, GDK, GDV, GCH, GTAU = 4, 128, 256, 64, 16.0
NCHUNK = SEQ // GCH
MH, QLORA, KVL, DR, DN = 8, 768, 256, 64, 128
QC = QLORA // P
MSCALE = float(DN + DR) ** -0.5
PH, NK, TOPK = 8, 128, 16
TROWS, TCOLS = 4, 4
TCAND = TROWS * TOPK + (TOPK - TROWS) * TCOLS
RING = 8
SLOT = 1024
TPG = 4
NBLK = N // 32
NPAGE = PAST // PAGE
HPAGES = NPAGE // 2

CONST = {}


def const_layout():
    at, out = 0, {}
    for name, n in (("ident", P), ("iota", P), ("chunk", P), ("chunk_s", NS_TOK), ("seqsel", DEC_B),
                    ("causal", P), ("causal_s", DEC_T), ("row_start", TOPK)):
        out[name] = (at, n)
        at += n
    return out, at


def constants():
    lay, n = const_layout()
    c = np.zeros((P, n), np.float32)
    p, j = np.arange(P)[:, None], np.arange(P)[None, :]
    put = lambda name, v: c.__setitem__((slice(0, v.shape[0]), slice(lay[name][0], sum(lay[name]))), v)
    put("ident", np.eye(P, dtype=np.float32))
    put("iota", np.broadcast_to(j, (P, P)).astype(np.float32))
    put("chunk", ((p <= j) & (p // GCH == j // GCH)).astype(np.float32))
    ps, js = p[:NS_TOK], j[:, :NS_TOK]
    put("chunk_s", ((ps <= js) & (ps // DEC_T == js // DEC_T)).astype(np.float32))
    put("seqsel", (ps // DEC_T == j[:, :DEC_B]).astype(np.float32))
    put("causal", np.where(j <= p, 0.0, NEG).astype(np.float32))
    put("causal_s", np.where(j[:, :DEC_T] <= ps % DEC_T, 0.0, NEG).astype(np.float32))
    a = np.arange(TOPK)
    put("row_start", np.broadcast_to(np.where(a < TROWS, a * TOPK, TROWS * TOPK + (a - TROWS) * TCOLS), (P, TOPK)).astype(np.float32))
    half = DR // 2
    inv = np.float32(10000.0) ** (-np.arange(half, dtype=np.float32) / np.float32(half))
    pos = np.concatenate([np.arange(SEQ), PAST + np.arange(NS_TOK) % DEC_T]).astype(np.float32)
    ang = (pos[:, None] * inv[None, :]).astype(np.float32)
    cos, sin = np.cos(ang).astype(np.float32), np.sin(ang).astype(np.float32)
    ct, st = np.zeros((NT * P, DR), np.float32), np.zeros((NT * P, DR), np.float32)
    ct[:N] = np.concatenate([cos, cos], 1)
    st[:N] = np.concatenate([-sin, sin], 1)
    rope_tok = np.stack([ct.reshape(NT, P, DR), st.reshape(NT, P, DR)]).transpose(2, 0, 1, 3).reshape(P, -1)
    cf = np.concatenate([cos.T] * 4, 0)
    sf = np.concatenate([sin.T, -sin.T] * 2, 0)
    rope_feat = np.concatenate([cf, sf], 1)
    return c, np.ascontiguousarray(rope_tok), np.ascontiguousarray(rope_feat)


class Steps:

    def __init__(self, eng, sem):
        self.eng, self.sem, self.n = eng, sem, 0

    def __call__(self, ins):
        self.n = self.n + 1
        ins.then_inc(self.sem, 1)
        self.eng.wait_ge(self.sem, self.n)


class Mark:

    def __init__(self, sem, base):
        self.sem, self.base = sem, base

    def __call__(self, n):
        return self.sem, n + self.base


class Ring:

    def __init__(self, buf, landed, used):
        self.buf, self.landed, self.used = buf, landed, used
        self.loaded = self.taken = 0

    def load(self, sp, src):
        n = self.loaded
        if n >= RING:
            sp.wait_ge(self.used, n - RING + 1)
        sp.dma_start(self.buf[:, n % RING, 0:src.shape[-1]], src).then_inc(self.landed[n % RING], 16)
        self.loaded = n + 1

    def load_loop(self, sp, srcs, first, count):
        base = self.loaded
        assert base >= RING or first >= 1
        with sp.Fori(first, count) as i:
            for j in range(RING):
                n = base + j
                sp.wait_ge(self.used, (i - first) * RING + (n - RING + 1))
                sp.dma_start(self.buf[:, n % RING, :], srcs(i, j)).then_inc(self.landed[n % RING], 16)
        self.loaded = base + (count - first) * RING

    def take(self, pe, turn=None, j=0):
        n = self.taken + j
        need = 16 * (n // RING + 1)
        pe.wait_ge(self.landed[n % RING], need if turn is None else turn * 16 + need)
        if turn is None:
            self.taken = n + 1
        return self.buf[:, n % RING, :]


class Arena:

    def __init__(self, buf, width):
        self.buf, self.width, self.at = buf, width, 0

    def __call__(self, *shape, at=None):
        n = int(np.prod(shape))
        if at is not None:
            self.at = at
        a = self.buf[:, self.at:self.at + n]
        self.at += n
        assert self.at <= self.width, (self.at, self.width)
        if len(shape) == 2:
            a = a.rearrange("p (a b) -> p a b", b=shape[1])
        elif len(shape) == 3:
            a = a.rearrange("p (a b c) -> p a b c", b=shape[1], c=shape[2])
        elif len(shape) == 4:
            a = a.rearrange("p (a b c d) -> p a b c d", b=shape[1], c=shape[2], d=shape[3])
        return a


def cols(tile, np_):
    return slice(tile * P, tile * P + np_)


def build(nc, d):
    ctx = ExitStack()
    with ctx:
        sb = lambda name, w, dt=F32: ctx.enter_context(nc.sbuf_tensor(name, [P, w], dt))
        sem = lambda name: ctx.enter_context(nc.semaphore(name))
        shared = {}
        turns_taken = sem("turns_taken")

        def alone(e):
            e.sem_inc(turns_taken, 1)

        def mark(name, per_use):
            handle, uses = shared.get(name, (None, 0))
            handle = handle or sem(name)
            shared[name] = (handle, uses + 1)
            return Mark(handle, uses * per_use)

        ring_buf = sb("ring", RING * SLOT)[:, :].rearrange("p (s c) -> p s c", c=SLOT)
        x = sb("x", NT * D)[:, :].rearrange("p (t c) -> p t c", c=D)
        hT = sb("hT", KC * N)[:, :].rearrange("p (k n) -> p k n", n=N)
        modT = sb("modT", 2 * 4 * KC * NSEQ)[:, :].rearrange("p (l w k s) -> p l w k s", l=2, w=4, s=NSEQ)
        lay, ncon = const_layout()
        con = sb("con", ncon)
        arena_w, exp_w = 34200, 7700
        with ExitStack() as over:
            over.enter_context(nc.sbuf_tensor("scratch_head", [P, exp_w], F32))
            r_sb = lambda name, *shape: over.enter_context(nc.sbuf_tensor(name, [P, *shape], F32R))
            hR, aR = r_sb("h_parts", 2, KC, N)[:], r_sb("a_parts", 2, TPG, N)[:]
            uR, vR = r_sb("u_parts", 2, 2, D)[:], r_sb("v_parts", TPG, 2, D)[:]
        arena_buf = sb("arena", arena_w)
        ps = ctx.enter_context(nc.psum_tensor("ps", [P, 8, 512], F32))
        K = {name: con[:, a:a + n] for name, (a, n) in lay.items()}
        ident = K["ident"]

        ring = Ring(ring_buf, [sem(f"slot{i}_landed") for i in range(RING)], sem("slots_used"))
        used = ring.used
        con_in, x_in, stage_over = sem("con_in"), sem("x_in"), sem("stage_over")
        dve_chain = Steps(nc.vector, sem("dve_step"))
        stages, plan = [], [0]

        def reserve(n):
            plan[0] += n
            return plan[0] - n

        def transpose(pe, out, in_):
            return pe.transpose(out, in_, ident[0:in_.shape[0], 0:in_.shape[0]])

        rows_made = sem("rows_made")
        rows_plan = [0]

        class RowProduct:

            def __init__(self, groups, first_slot):
                self.base, self.first_slot = rows_plan[0], first_slot
                rows_plan[0] += 4 * groups
                self.slots = {}

            def tile(self, pe, t, src, bank):
                np_ = TILES[t][1]
                for s in range(4):
                    if t == 0:
                        self.slots[s] = ring.take(pe)
                    for kk in range(2):
                        k = 2 * s + kk
                        mm = pe.matmul(ps[0:np_, bank, :], src[:, k, cols(t, np_)], self.slots[s][:, kk * 512:(kk + 1) * 512],
                                       start=(k == 0), stop=(k == KC - 1))
                    if t == NT - 1:
                        mm.then_inc(used, 1)
                if t < NT - 1:
                    mm.then_inc(rows_made, 1)

            def group(self, pe, src, bank_of, before):
                for t in range(NT):
                    before(t)
                    self.tile(pe, t, src, bank_of(t))

            def wait(self, e, g, t):
                if t < NT - 1:
                    e.wait_ge(rows_made, self.base + 4 * g + t + 1)
                else:
                    e.wait_ge(used, self.first_slot + 4 * (g + 1))

        def pair(b):
            return ps[:, b:b + 2, 0:HALF]

        def halves(a):
            return a.rearrange("p (h n) -> p h n", h=2)

        def stage_ada():
            A = Arena(arena_buf, arena_w)
            G6 = 12
            rows, bias = A(G6 * D), A(G6 * D)
            cT = A(KC, NSEQ)
            condT = A(KC, NSEQ)
            base = reserve(G6 * RING)
            c_in, bias_in, cond_ready = sem("c_in"), sem("ada_bias_in"), sem("cond_ready")
            row_done, rows_saved = sem("mod_row_done"), sem("mod_rows_saved")
            colT_ps, colT_done = sem("modT_ps"), sem("modT_done")

            def sp(e):
                e.dma_start(con[:, :], d["con"]).then_inc(con_in, 16)
                e.dma_start(cT, d["cT"]).then_inc(c_in, 16)
                for j in range(RING):
                    ring.load(e, d["ada_w"][j])
                for t, np_ in TILES:
                    e.dma_start(x[0:np_, t, :], d["x"][t * P:t * P + np_, :]).then_inc(x_in, 16)
                ring.load_loop(e, lambda i, j: d["ada_w"][i * RING + j], 1, G6)

            def pool(e):
                e.dma_start(bias[0:NSEQ], d["ada_b"].broadcast_to([NSEQ, G6 * D])).then_inc(bias_in, 16)
                e.wait_ge(row_done, G6 + 2)
                e.dma_start(d["mod"], rows[0:NSEQ]).then_inc(rows_saved, 16)
                e.wait_ge(rows_saved, 16)

            def act(e):
                e.wait_ge(c_in, 16)
                e.activation(condT, cT, ACT.Silu).then_inc(cond_ready, 1)

            def pe(e):
                e.wait_ge(cond_ready, 1)
                with e.Fori(0, G6 // 2) as i:
                    for u in range(2):
                        e.wait_ge(row_done, i * 2 + (u + 1))
                        for k in range(KC):
                            n = u * RING + k
                            e.wait_ge(ring.landed[k], i * 32 + 16 * (u + 1))
                            for h in range(2):
                                mm = e.matmul(ps[0:NSEQ, 2 * u + h, :], condT[:, k, :],
                                              ring_buf[:, k, h * 512:(h + 1) * 512], start=(k == 0), stop=(k == KC - 1))
                            mm.then_inc(used, 1)
                ring.taken = G6 * RING
                e.wait_ge(row_done, G6 + 2)
                e.wait_ge(con_in, 16)
                for l in range(2):
                    for w, q in enumerate((0, 1, 3, 4)):
                        for k in range(KC):
                            o = (w * KC + k) * NSEQ
                            src = (l * 6 + q) * D + k * P
                            mm = transpose(e, ps[:, 4 + l, o:o + NSEQ], rows[0:NSEQ, src:src + P])
                    mm.then_inc(colT_ps, 1)

            def dve(e):
                e.wait_ge(bias_in, 16)
                e.sem_inc(row_done, 2)
                with e.Fori(0, G6 // 2) as i:
                    for u in range(2):
                        e.wait_ge(used, i * 16 + 8 * (u + 1))
                        o = bass.ds((i * 2 + u) * D, D)
                        e.tensor_tensor(rows[0:NSEQ, o], ps[0:NSEQ, 2 * u:2 * u + 2, :].rearrange("p a b -> p (a b)"),
                                        bias[0:NSEQ, o], ALU.add).then_inc(row_done, 1)
                for l in range(2):
                    e.wait_ge(colT_ps, l + 1)
                    v = ps[:, 4 + l, 0:4 * KC * NSEQ].rearrange("p (w r) -> p w r", w=4)
                    o = modT[:, l].rearrange("p w k s -> p w (k s)")
                    e.tensor_copy(o[:, 0:4:2], v[:, 0:4:2]).then_inc(colT_done, 1)
                    e.tensor_scalar(o[:, 1:4:2], v[:, 1:4:2], 1.0, None, ALU.add).then_inc(colT_done, 1)

            return sp, pe, act, dve, pool

        def stage_modulate(l, which):
            A = Arena(arena_buf, arena_w)
            tmp = A(KC, DEC_B, DEC_T)
            xT_ps, hT_done, tmp_done = mark("xT_ps", KC + 1), mark("hT_done", KC), mark("hT_tmp", 2)
            shift, scale = modT[:, l, 2 * which], modT[:, l, 2 * which + 1]

            def sp(e):
                pass

            def pe(e):
                e.wait_ge(x_in, 16 * NT)
                for k in range(KC):
                    if k >= 4:
                        e.wait_ge(*hT_done(k - 3))
                    for t in range(4):
                        mm = transpose(e, ps[:, k % 4, t * P:(t + 1) * P], x[:, t, k * P:(k + 1) * P])
                    mm.then_inc(xT_ps.sem, 1)
                for k in range(KC):
                    mm = transpose(e, ps[:, 4, k * NS_TOK:(k + 1) * NS_TOK], x[0:NS_TOK, 4, k * P:(k + 1) * P])
                mm.then_inc(xT_ps.sem, 1)

            def act(e):
                for k in range(KC):
                    e.wait_ge(*xT_ps(k + 1))
                    e.activation(hT[:, k, 0:SEQ], ps[:, k % 4, :], ACT.Identity,
                                 bias=shift[:, k, 0:1], scale=scale[:, k, 0:1]).then_inc(hT_done.sem, 1)

            def dve(e):
                e.wait_ge(*xT_ps(KC + 1))
                v = ps[:, 4, 0:KC * NS_TOK].rearrange("p (k s t) -> p k s t", k=KC, t=DEC_T)
                spread = lambda m: m[:, :, 1:].unsqueeze(3).broadcast_to([P, KC, DEC_B, DEC_T])
                e.tensor_tensor(tmp, v, spread(scale), ALU.mult).then_inc(tmp_done.sem, 1)
                e.wait_ge(*tmp_done(1))
                o = hT[:, :, SEQ:N].rearrange("p k (s t) -> p k s t", t=DEC_T)
                e.tensor_tensor(o, tmp, spread(shift), ALU.add).then_inc(tmp_done.sem, 1)

            return sp, pe, act, dve, lambda e: None

        def stage_close(l, which, w_o=None, yT=None):
            A = Arena(arena_buf, arena_w)
            if yT is not None:
                A.at = KC * N
            gate = A(2, D)
            lng, lnb = A(D), A(D)
            z = A(2, 512)
            st, mv = A(NT, 2, 6), A(NT, 2)
            rstd, shift = A(NT), A(NT)
            rows_in, z_ready, var_ready, std_ready, coef_ready, x_std, x_gained = (mark(*s) for s in (
                ("gate_rows_in", 64), ("out_gated", 2 * NT), ("var_ready", NT), ("std_ready", NT), ("norm_coef", NT),
                ("x_standard", NT), ("x_gained", NT)))
            tps = mark("y_tok_ps", NT) if yT is not None else None
            out_rows = RowProduct(2, reserve(8)) if w_o is not None else None
            y0 = (l * 6 + (5 if which else 2)) * D

            def sp(e):
                if w_o is not None:
                    for s in range(8):
                        ring.load(e, d[w_o][s])

            def pool(e):
                e.dma_start(gate[:, 0], d["mod"][0:1, y0:y0 + D].broadcast_to([P, D])).then_inc(rows_in.sem, 16)
                e.dma_start(gate[0:NS_TOK, 1], d["mod"][1:NSEQ, y0:y0 + D].unsqueeze(1).broadcast_to(
                    [DEC_B, DEC_T, D])).then_inc(rows_in.sem, 16)
                r = 2 * l + which
                e.dma_start(lng, d["ln_g"][r:r + 1, :].broadcast_to([P, D])).then_inc(rows_in.sem, 16)
                e.dma_start(lnb, d["ln_b"][r:r + 1, :].broadcast_to([P, D])).then_inc(rows_in.sem, 16)
                e.wait_ge(*rows_in(64))
                for t, np_ in TILES:
                    e.wait_ge(*x_gained(t + 1))
                    e.tensor_tensor(x[0:np_, t], x[0:np_, t], lnb[0:np_], ALU.add)

            def pe(e):
                if w_o is not None:
                    for g in range(2):
                        def bank_free(t):
                            if g and t >= 3:
                                e.wait_ge(*z_ready(t - 2))
                        out_rows.group(e, hT, lambda t: (5 * g + t) % 8, bank_free)
                else:
                    for t, np_ in TILES:
                        if t == 4:
                            e.wait_ge(*z_ready(2))
                        for k in range(KC):
                            mm = transpose(e, ps[0:np_, 2 * (t % 4) + k // 4, (k % 4) * P:(k % 4 + 1) * P], yT[:, k, cols(t, np_)])
                        mm.then_inc(tps.sem, 1)

            def act(e):
                for t, np_ in TILES:
                    e.wait_ge(*var_ready(t + 1))
                    e.activation(rstd[0:np_, t:t + 1], rstd[0:np_, t:t + 1], ACT.Sqrt).then_inc(std_ready.sem, 1)
                    e.wait_ge(*coef_ready(t + 1))
                    e.activation(x[0:np_, t], x[0:np_, t], ACT.Identity, bias=shift[0:np_, t:t + 1],
                                 scale=rstd[0:np_, t:t + 1]).then_inc(x_std.sem, 1)

            def dve(e):
                D_ = dve_chain
                gated = [0]

                def residual(t, np_, g):
                    if w_o is not None:
                        out_rows.wait(e, g, t)
                        b = (5 * g + t) % 8
                    else:
                        e.wait_ge(*tps(t + 1))
                        b = 2 * (t % 4) + g
                    i = gated[0]
                    gated[0] += 1
                    c = slice(g * 512, (g + 1) * 512)
                    e.tensor_tensor(z[0:np_, i % 2], ps[0:np_, b, :], gate[0:np_, t // 4, c], ALU.mult).then_inc(z_ready.sem, 1)
                    e.wait_ge(*z_ready(i + 1))
                    D_(e.scalar_tensor_tensor(out=x[0:np_, t, c], in0=x[0:np_, t, c], scalar=ALPHA,
                                              in1=z[0:np_, i % 2], op0=ALU.mult, op1=ALU.add))

                def statistics(t, np_):
                    r, one = slice(0, np_), slice(t, t + 1)
                    for g in range(2):
                        ins = e.bn_stats(st[r, t, g], x[r, t, g * 512:(g + 1) * 512])
                    D_(ins)
                    D_(e.bn_aggr(mv[r, t], st[r, t].rearrange("p a b -> p (a b)")))
                    e.tensor_scalar(rstd[r, one], mv[r, t, 1:2], LN_EPS, None, ALU.add).then_inc(var_ready.sem, 1)

                def coefficients(t, np_):
                    r, one = slice(0, np_), slice(t, t + 1)
                    e.wait_ge(*std_ready(t + 1))
                    D_(e.reciprocal(rstd[r, one], rstd[r, one]))
                    e.tensor_scalar(shift[r, one], mv[r, t, 0:1], rstd[r, one], -1.0, ALU.mult, ALU.mult).then_inc(coef_ready.sem, 1)

                def gain(t, np_):
                    e.wait_ge(*x_std(t + 1))
                    e.tensor_tensor(x[0:np_, t], x[0:np_, t], lng[0:np_], ALU.mult).then_inc(x_gained.sem, 1)

                e.wait_ge(*rows_in(64))
                if w_o is not None:
                    for t, np_ in TILES:
                        residual(t, np_, 0)
                for t, np_ in TILES:
                    if w_o is None:
                        residual(t, np_, 0)
                    residual(t, np_, 1)
                    statistics(t, np_)
                    if t:
                        gain(*TILES[t - 1])
                    coefficients(t, np_)
                gain(*TILES[-1])

            return sp, pe, act, dve, pool

        def stage_gla():
            A = Arena(arena_buf, arena_w)
            qk = A(2 * GH, N)
            expB = A(GH, N)
            Bc = A(GH, N)
            ke = A(GH, N)
            states = A(3, GH * GDV, at=qk.shape[1] * N)
            onorm = A(D)
            A.at = 5 * GH * N
            gtok = A(NT, GH * GDK)
            vtok, rtok = A(NT, D), A(NT, D)
            attT = A(2, GH * P)
            S0 = A(2, DEC_B * GDV)
            kem = A(DEC_B, GDK)
            qsel = A(GH, DEC_B * NS_TOK)
            tmpA = A(512)
            wgl = A(KC, 16)
            wg2 = A(GH * GDK)
            glT = A(N)
            normg = A(GDV)
            st, mv = A(GH, 6), A(GH, 2)
            rstd = A(GH)
            last, last_s = A(GH, NCHUNK), A(GH, DEC_B)
            base = reserve(24)
            vr = RowProduct(4, base + 8)
            small_in = sem("gla_small_in")
            qk_done, gl_ps, gl_done = sem("qk_done"), sem("gl_ps"), sem("gl_done")
            g_ps, lsp_done, g_done = sem("g_ps"), sem("lsp_done"), sem("g_done")
            B_ps, B_done, D_done, exp_done, kd_done = sem("B_ps"), sem("B_done"), sem("D_done"), sem("exp_done"), sem("kd_done")
            vr_done, ket_ps, ket_done = sem("vr_done"), sem("ket_ps"), sem("ket_done")
            att_ps, att_done, ds_ps, ds_done = sem("att_ps"), sem("att_done"), sem("ds_ps"), sem("ds_done")
            o_ps, o_read, ovar, ostd, on_done, oT_ps, oT_done = (sem(s) for s in (
                "o_ps", "o_read", "o_var", "o_std", "on_done", "oT_ps", "oT_done"))
            S0_in, qsel_done, kem_done, s_out = [sem("S0_in0"), sem("S0_in1")], sem("qsel_done"), sem("kem_done"), [sem("S_out0"), sem("S_out1")]
            sp_out, state_zero = sem("gla_state_out"), sem("att_zero")
            bank_vr = lambda g, t: (5 * g + t) % 8

            def sp(e):
                for s in range(24):
                    ring.load(e, d["gla_w"][s])

            def pool(e):
                e.dma_start(wgl, d["gla_wgl"]).then_inc(small_in, 16)
                e.dma_start(wg2[0:17], d["gla_wg2"]).then_inc(small_in, 16)
                e.dma_start(normg, d["gla_norm_g"].broadcast_to([P, GDV])).then_inc(small_in, 16)
                for h in range(2):
                    e.dma_start(S0[:, h].rearrange("p (b v) -> p b v", b=DEC_B), d["state_gla"][:, h].rearrange("b k v -> k b v")).then_inc(S0_in[h], 16)
                e.wait_ge(ds_done, NCHUNK)
                e.dma_start(d["o_gla_p"].rearrange("h k v -> k h v"),
                            states[:, NCHUNK % 3].rearrange("p (h v) -> p h v", h=GH)).then_inc(sp_out, 16)
                for h in range(GH):
                    e.wait_ge(ds_done, NCHUNK + 4 * (h + 1))
                    v = S0[:, h % 2].rearrange("p (b v) -> p b v", b=DEC_B)
                    e.dma_start(d["o_gla_s"][:, h].rearrange("b k v -> k b v"), v).then_inc(s_out[h % 2], 16)
                    e.wait_ge(s_out[h % 2], 16 * (h // 2 + 1))
                    if h + 2 < GH:
                        e.dma_start(v, d["state_gla"][:, h + 2].rearrange("b k v -> k b v")).then_inc(S0_in[h % 2], 16)
                e.wait_ge(sp_out, 16)

            def pe(e):
                e.wait_ge(small_in, 48)
                for m in range(2 * GH):
                    slot = ring.take(e)
                    if m >= 2:
                        e.wait_ge(qk_done, m - 1)
                    for h in range(2):
                        for k in range(KC):
                            mm = e.matmul(ps[:, 2 * (m % 2) + h, 0:HALF], slot[:, k * P:(k + 1) * P],
                                          hT[:, k, h * HALF:(h + 1) * HALF], start=(k == 0), stop=(k == KC - 1))
                    mm.then_inc(used, 1)
                for h in range(2):
                    for k in range(KC):
                        mm = e.matmul(ps[0:16, 4 + h, 0:HALF], wgl[:, k, :], hT[:, k, h * HALF:(h + 1) * HALF],
                                      start=(k == 0), stop=(k == KC - 1))
                mm.then_inc(gl_ps, 1)
                e.wait_ge(gl_done, 2)
                e.wait_ge(qk_done, 8)
                for t, np_ in TILES:
                    e.matmul(ps[0:np_, t, :], glT[0:17, cols(t, np_)], wg2[0:17], start=True, stop=True).then_inc(g_ps, 1)
                for t, np_ in TILES:
                    e.wait_ge(g_done, t + 1)
                    m = K["chunk"] if t < 4 else K["chunk_s"][0:NS_TOK]
                    for h in range(GH):
                        mm = e.matmul(ps[:, t, h * P:h * P + np_], gtok[0:np_, t, h * P:(h + 1) * P], m, start=True, stop=True)
                    mm.then_inc(B_ps, 1)
                e.wait_ge(B_done, NT)
                for g in range(4):
                    def bank_free(t):
                        if 5 * g + t >= 8:
                            e.wait_ge(vr_done, 5 * g + t - 7)
                    vr.group(e, hT, lambda t: bank_vr(g, t), bank_free)
                e.wait_ge(kd_done, 4)
                e.wait_ge(vr_done, 20)
                for t, np_ in TILES:
                    for h in range(GH):
                        mm = transpose(e, ps[0:np_, t, h * P:(h + 1) * P], ke[:, h, cols(t, np_)])
                    mm.then_inc(ket_ps, 1)
                e.wait_ge(ket_done, NT)

                def out_tile(t, np_):
                    e.wait_ge(on_done, t + 1)
                    if t:
                        e.wait_ge(oT_done, t)
                    for k in range(KC):
                        mm = transpose(e, ps[:, k // 4, (k % 4) * P:(k % 4) * P + np_], onorm[0:np_, k * P:(k + 1) * P])
                    mm.then_inc(oT_ps, 1)

                for t in range(4):
                    for h in range(GH):
                        mm = e.matmul(ps[:, 5, h * P:(h + 1) * P], qk[:, GH + h, cols(t, P)], qk[:, h, cols(t, P)], start=True, stop=True)
                    mm.then_inc(att_ps, 1)
                    for u in range(2):
                        n = 2 * t + u
                        r = slice(u * GCH, (u + 1) * GCH)
                        if n:
                            e.wait_ge(ds_done, n)
                        for h in range(GH):
                            mm = e.matmul(ps[:, 6 + h // 2, (h % 2) * GDV:(h % 2 + 1) * GDV], gtok[r, t, h * P:(h + 1) * P],
                                          vtok[r, t, h * GDV:(h + 1) * GDV], start=True, stop=True)
                        mm.then_inc(ds_ps, 1)
                    e.wait_ge(att_done, t + 1)
                    e.wait_ge(ds_done, 2 * t + 1)
                    if t:
                        e.wait_ge(o_read, t)
                    for h in range(GH):
                        o = ps[:, 2 + h // 2, (h % 2) * GDV:(h % 2 + 1) * GDV]
                        mm = e.matmul(o, attT[:, t % 2, h * P:(h + 1) * P], vtok[:, t, h * GDV:(h + 1) * GDV],
                                      start=True, stop=False, skip_group_check=True)
                        for u in range(2):
                            n = 2 * t + u
                            if n:
                                mm = e.matmul(o[u * GCH:(u + 1) * GCH], qk[:, h, n * GCH:(n + 1) * GCH],
                                              states[:, n % 3, h * GDV:(h + 1) * GDV], start=False, stop=(u == 1), skip_group_check=True)
                    mm.then_inc(o_ps, 1)
                    if t:
                        out_tile(t - 1, P)
                for h in range(GH):
                    mm = e.matmul(ps[0:NS_TOK, 5, h * P:h * P + NS_TOK], qk[:, GH + h, SEQ:N], qk[:, h, SEQ:N], start=True, stop=True)
                mm.then_inc(att_ps, 1)
                e.wait_ge(att_done, 5)
                e.wait_ge(qsel_done, 2)
                e.wait_ge(o_read, 4)
                for h in range(GH):
                    o = ps[0:NS_TOK, 2 + h // 2, (h % 2) * GDV:(h % 2 + 1) * GDV]
                    e.matmul(o, attT[0:NS_TOK, 0, h * P:h * P + NS_TOK], vtok[0:NS_TOK, 4, h * GDV:(h + 1) * GDV],
                             start=True, stop=False, skip_group_check=True)
                    e.wait_ge(S0_in[h % 2], 16 * (h // 2 + 1))
                    for b in range(DEC_B):
                        mm = e.matmul(o, qsel[:, h, b * NS_TOK:(b + 1) * NS_TOK], S0[:, h % 2, b * GDV:(b + 1) * GDV],
                                      start=False, stop=(b == DEC_B - 1), skip_group_check=True)
                    mm.then_inc(o_ps, 1)
                    e.wait_ge(kem_done, h + 1)
                    for q in range(4):
                        n = 4 * h + q
                        e.wait_ge(ds_done, NCHUNK + n - 1) if n else e.wait_ge(ds_done, NCHUNK)
                        for b in (2 * q, 2 * q + 1):
                            mm = e.matmul(ps[:, 6 + n % 2, (b % 2) * GDV:(b % 2 + 1) * GDV], kem[0:NS_TOK, b, :],
                                          vtok[0:NS_TOK, 4, h * GDV:(h + 1) * GDV], start=True, stop=True)
                        mm.then_inc(ds_ps, 1)
                    if h == 0:
                        out_tile(3, P)
                out_tile(4, NS_TOK)

            def act(e):
                S_ = Steps(e, sem("gla_act_step"))
                for m in range(2 * GH):
                    e.wait_ge(used, base + m + 1)
                    e.activation(halves(qk[:, m, :]), pair(2 * (m % 2)), ACT.Copy,
                                 scale=GDK ** -0.5 if m < GH else 1.0).then_inc(qk_done, 1)
                for t, np_ in TILES:
                    e.wait_ge(g_ps, t + 1)
                    if t:
                        e.wait_ge(g_done, t)
                    S_(e.activation(tmpA[0:np_], ps[0:np_, t, :], ACT.Abs))
                    S_(e.activation(tmpA[0:np_], tmpA[0:np_], ACT.Exp, scale=-1.0))
                    e.activation(tmpA[0:np_], tmpA[0:np_], ACT.Ln, bias=1.0).then_inc(lsp_done, 1)
                e.wait_ge(B_done, NT)
                e.activation(expB, Bc, ACT.Exp, scale=1.0 / GTAU).then_inc(exp_done, 1)
                e.wait_ge(D_done, 2)
                e.activation(ke, ke, ACT.Exp, scale=1.0 / GTAU).then_inc(exp_done, 1)
                e.activation(Bc, Bc, ACT.Exp, scale=-1.0 / GTAU).then_inc(exp_done, 1)
                for g in range(4):
                    for t, np_ in TILES:
                        vr.wait(e, g, t)
                        o = (vtok if g < 2 else rtok)[0:np_, t, (g % 2) * 512:(g % 2 + 1) * 512]
                        e.activation(o, ps[0:np_, bank_vr(g, t), :], ACT.Copy if g < 2 else ACT.Silu).then_inc(vr_done, 1)
                for t, np_ in TILES:
                    e.wait_ge(ovar, t + 1)
                    e.activation(rstd[0:np_], rstd[0:np_], ACT.Sqrt).then_inc(ostd, 1)
                    e.wait_ge(oT_ps, t + 1)
                    v = ps[:, 0:2, :].rearrange("p b (k n) -> p (b k) n", k=4)
                    e.activation(hT[:, :, cols(t, np_)], v[:, :, 0:np_], ACT.Copy).then_inc(oT_done, 1)

            def dve(e):
                S_ = dve_chain
                S_(e.memset(glT[0:17], 1.0))
                S_(e.memset(qsel, 0.0))
                S_(e.memset(attT, 0.0))
                e.wait_ge(gl_ps, 1)
                e.tensor_copy(halves(glT[0:16]), ps[0:16, 4:6, 0:HALF]).then_inc(gl_done, 2)
                for t, np_ in TILES:
                    e.wait_ge(lsp_done, t + 1)
                    e.scalar_tensor_tensor(out=gtok[0:np_, t], in0=ps[0:np_, t, :], scalar=0.0, in1=tmpA[0:np_],
                                           op0=ALU.min, op1=ALU.subtract).then_inc(g_done, 1)
                for t, np_ in TILES:
                    e.wait_ge(B_ps, t + 1)
                    v = ps[:, t, :].rearrange("p (h n) -> p h n", h=GH)[:, :, 0:np_]
                    e.tensor_copy(Bc[:, :, cols(t, np_)], v).then_inc(B_done, 1)
                e.wait_ge(B_done, NT)
                for a, c, w in ((0, NCHUNK, GCH), (SEQ, DEC_B, DEC_T)):
                    v = Bc[:, :, a:a + c * w].rearrange("p h (c w) -> p h c w", w=w)
                    o = ke[:, :, a:a + c * w].rearrange("p h (c w) -> p h c w", w=w)
                    for h in range(GH):
                        ins = e.tensor_tensor(o[:, h], v[:, h, :, w - 1:w].broadcast_to([P, c, w]), v[:, h], ALU.subtract)
                    ins.then_inc(D_done, 1)
                e.wait_ge(exp_done, 1)
                f = lambda a: a.rearrange("p h n -> p (h n)")
                S_(e.tensor_tensor(f(qk[:, 0:GH]), f(qk[:, 0:GH]), f(expB), ALU.mult))
                e.tensor_copy(last, expB[:, :, GCH - 1:SEQ:GCH]).then_inc(kd_done, 1)
                e.tensor_copy(last_s, expB[:, :, SEQ + DEC_T - 1:N:DEC_T]).then_inc(kd_done, 1)
                e.wait_ge(exp_done, 2)
                e.tensor_tensor(f(ke), f(ke), f(qk[:, GH:]), ALU.mult).then_inc(kd_done, 1)
                e.wait_ge(exp_done, 3)
                e.tensor_tensor(f(qk[:, GH:]), f(qk[:, GH:]), f(Bc), ALU.mult).then_inc(kd_done, 1)
                e.wait_ge(kd_done, 4)
                for h in range(GH):
                    v = qsel[:, h].rearrange("p (b r) -> p b r", b=DEC_B)
                    for b in range(DEC_B):
                        ins = e.tensor_copy(v[:, b, b * DEC_T:(b + 1) * DEC_T], qk[:, h, SEQ + b * DEC_T:SEQ + (b + 1) * DEC_T])
                ins.then_inc(qsel_done, 2)
                for t, np_ in TILES:
                    e.wait_ge(ket_ps, t + 1)
                    e.tensor_copy(gtok[0:np_, t], ps[0:np_, t, :]).then_inc(ket_done, 1)

                def normalise(t, np_):
                    o = lambda h: ps[0:np_, 2 + h // 2, (h % 2) * GDV:(h % 2 + 1) * GDV]
                    e.wait_ge(o_ps, t + 1 if t < 4 else 8)
                    for h in range(GH):
                        ins = e.bn_stats(st[0:np_, h], o(h))
                    S_(ins)
                    for h in range(GH):
                        ins = e.bn_aggr(mv[0:np_, h], st[0:np_, h])
                    S_(ins)
                    e.tensor_scalar(rstd[0:np_], mv[0:np_, :, 1], LN_EPS, None, ALU.add).then_inc(ovar, 1)
                    e.wait_ge(ostd, t + 1)
                    S_(e.reciprocal(rstd[0:np_], rstd[0:np_]))
                    if t:
                        e.wait_ge(oT_ps, t)
                    for h in range(GH):
                        ins = e.tensor_scalar(onorm[0:np_, h * GDV:(h + 1) * GDV], o(h), mv[0:np_, h, 0:1], rstd[0:np_, h:h + 1],
                                              ALU.subtract, ALU.mult)
                    ins.then_inc(o_read, 1)
                    e.wait_ge(o_read, t + 1)
                    v = onorm[0:np_].rearrange("p (h v) -> p h v", h=GH)
                    S_(e.tensor_tensor(v, v, normg[0:np_].unsqueeze(1).broadcast_to([np_, GH, GDV]), ALU.mult))
                    e.wait_ge(vr_done, 20)
                    e.tensor_tensor(onorm[0:np_], onorm[0:np_], rtok[0:np_, t], ALU.mult).then_inc(on_done, 1)

                def mask_att(t, np_):
                    e.wait_ge(att_ps, t + 1)
                    if t >= 2:
                        e.wait_ge(o_ps, t - 1)
                    m = (K["chunk"] if t < 4 else K["chunk_s"][0:NS_TOK]).bitcast(I32)
                    for h in range(GH):
                        s = slice(h * P, h * P + np_)
                        ins = e.copy_predicated(attT[0:np_, t % 2, s], m, ps[0:np_, 5, s])
                    ins.then_inc(att_done, 1)

                for t in range(4):
                    mask_att(t, P)
                    for u in range(2):
                        n = 2 * t + u
                        e.wait_ge(ds_ps, n + 1)
                        if n >= 2:
                            e.wait_ge(o_ps, (n - 2) // 2 + 1)
                        for h in range(GH):
                            c = slice(h * GDV, (h + 1) * GDV)
                            dS = ps[:, 6 + h // 2, (h % 2) * GDV:(h % 2 + 1) * GDV]
                            if n:
                                ins = e.scalar_tensor_tensor(out=states[:, (n + 1) % 3, c], in0=states[:, n % 3, c],
                                                             scalar=last[:, h, n:n + 1], in1=dS, op0=ALU.mult, op1=ALU.add)
                            else:
                                ins = e.tensor_copy(states[:, 1, c], dS)
                        ins.then_inc(ds_done, 1)
                        e.wait_ge(ds_done, n + 1)
                    normalise(t, P)
                e.wait_ge(o_ps, 3)
                S_(e.memset(attT[:, 0], 0.0))
                mask_att(4, NS_TOK)
                for h in range(GH):
                    if h:
                        e.wait_ge(ds_ps, NCHUNK + 4 * h)
                    for b in range(DEC_B):
                        ins = e.tensor_scalar(kem[0:NS_TOK, b], gtok[0:NS_TOK, 4, h * P:(h + 1) * P], K["seqsel"][0:NS_TOK, b:b + 1],
                                              None, ALU.mult)
                    ins.then_inc(kem_done, 1)
                    e.wait_ge(S0_in[h % 2], 16 * (h // 2 + 1))
                    for q in range(4):
                        n = 4 * h + q
                        e.wait_ge(ds_ps, NCHUNK + n + 1)
                        for b in (2 * q, 2 * q + 1):
                            s = S0[:, h % 2, b * GDV:(b + 1) * GDV]
                            ins = e.scalar_tensor_tensor(out=s, in0=s, scalar=last_s[:, h, b:b + 1],
                                                         in1=ps[:, 6 + n % 2, (b % 2) * GDV:(b % 2 + 1) * GDV], op0=ALU.mult, op1=ALU.add)
                        ins.then_inc(ds_done, 1)
                normalise(4, NS_TOK)

            return sp, pe, act, dve, pool

        def stage_search(l):
            A = Arena(arena_buf, arena_w)
            slotT = A(3, N)
            qn = A(2, 512)
            qT = A(2, 512)
            s1, s2 = A(2, 512), A(4, NK)
            keyT = A(2, NK)
            V, If, col, place = A(4, TOPK), A(2, 4, TOPK), A(2, TOPK), A(2, TOPK)
            Iu, Ju, mask = A(4, TOPK), A(2, TOPK), A(2, TOPK)
            step1 = A(2, TOPK)
            cand, cand2 = A(2, TCAND), A(2, TCAND)
            eq = A(2, 2, 2 * TOPK * TOPK)
            E1, E2, G = A(NT, P), A(NT, P), A(NT, P)
            gd, gs = A(NT, P), A(NT, PH)
            st, mv, rstd, shift = A(2, 6), A(2, 2, 2), A(2, 2), A(2, 2)
            Iu, Ju, mask = Iu.bitcast(U32), Ju.bitcast(U32), mask.bitcast(U32)
            q_rows = RowProduct(4, reserve(16))
            ITEMS = [(g, t, np_) for g in range(4) for t, np_ in TILES]
            last = len(ITEMS) - 1
            keys_in, slot_ps, slot_done = mark("keys_in", 16), mark("slot_ps", 1), mark("slotT_done", 2)
            qvar, qstd, qcoef, qn_done, qT_ps, qT_done, sc_ps, sc_done, s1_used, eq_done, eq_used, top_done = (mark(s, 4 * NT) for s in (
                "q_var", "q_std", "q_coef", "qn_done", "qT_ps", "qT_done", "score_ps", "score_done", "scores_ranked",
                "place_onehot", "place_times_key", "top_done"))
            diff_done, gexp_done, gates_done = (mark(s, NT) for s in ("gate_diff", "gate_exp", "gates_done"))

            def sp(e):
                for s in range(16):
                    ring.load(e, d["peer_wq"][l, s])

            def pool(e):
                e.dma_start(keyT, d["peer_keyT"][l]).then_inc(keys_in.sem, 16)
                for n, (g, t, np_) in enumerate(ITEMS):
                    r = slice(0, np_)
                    e.wait_ge(*eq_done(n + 1))
                    ev = eq[r, n % 2].rearrange("p w (h a b) -> p w h a b", h=2, a=TOPK)
                    sh = [np_, TOPK, TOPK]
                    for h in range(2):
                        e.tensor_tensor(ev[:, 0, h], ev[:, 0, h], step1[r, h].unsqueeze(1).broadcast_to(sh), ALU.mult)
                        ins = e.tensor_tensor(ev[:, 1, h], ev[:, 1, h], If[r, n % 2, 2 * h + 1].unsqueeze(1).broadcast_to(sh), ALU.mult)
                    ins.then_inc(eq_used.sem, 1)

            def pe(e):
                def queries(n):
                    if n >= NT:
                        e.wait_ge(*qn_done(n - NT + 1))
                    q_rows.tile(e, n % NT, hT, n % NT)

                e.wait_ge(*keys_in(16))
                queries(0)
                for n, (g, t, np_) in enumerate(ITEMS):
                    if n < last:
                        queries(n + 1)
                    e.wait_ge(*qn_done(n + 1))
                    if n:
                        e.wait_ge(*qT_done(n))
                    for j in range(4):
                        mm = transpose(e, ps[:, 5, j * P:j * P + np_], qn[0:np_, n % 2, j * P:(j + 1) * P])
                    mm.then_inc(qT_ps.sem, 1)
                    e.wait_ge(*qT_done(n + 1))
                    if n >= 2:
                        e.wait_ge(*sc_done(n - 1))
                    for j in range(4):
                        mm = e.matmul(ps[0:np_, 6 + n % 2, j * P:(j + 1) * P], qT[:, n % 2, j * P:j * P + np_], keyT[:, j % 2],
                                      start=True, stop=True)
                    mm.then_inc(sc_ps.sem, 1)
                e.wait_ge(*gates_done(NT))
                for w, src in enumerate((E1, E2, G)):
                    for t, np_ in TILES:
                        o = ps[:, w, cols(t, np_)] if t < 4 else ps[:, 3, w * NS_TOK:(w + 1) * NS_TOK]
                        mm = transpose(e, o, src[0:np_, t])
                mm.then_inc(slot_ps.sem, 1)

            def act(e):
                def deviation(n):
                    r, v = slice(0, ITEMS[n][2]), n % 2
                    e.wait_ge(*qvar(n + 1))
                    e.activation(rstd[r, v], rstd[r, v], ACT.Sqrt).then_inc(qstd.sem, 1)

                def standardise(n):
                    g, t, np_ = ITEMS[n]
                    r, v = slice(0, np_), n % 2
                    e.wait_ge(*qcoef(n + 1))
                    if n >= 2:
                        e.wait_ge(*qT_ps(n - 1))
                    for h in range(2):
                        c = slice(h * 256, (h + 1) * 256)
                        ins = e.activation(qn[r, v, c], ps[r, t, c], ACT.Identity, bias=shift[r, v, h:h + 1], scale=rstd[r, v, h:h + 1])
                    ins.then_inc(qn_done.sem, 1)

                for n, (g, t, np_) in enumerate(ITEMS):
                    deviation(n)
                    standardise(n)
                    e.wait_ge(*qT_ps(n + 1))
                    v = lambda a: a.rearrange("p (j n) -> p j n", j=4)[:, :, 0:np_]
                    e.activation(v(qT[:, n % 2]), v(ps[:, 5, :]), ACT.Copy).then_inc(qT_done.sem, 1)
                    e.wait_ge(*sc_ps(n + 1))
                    if n >= 2:
                        e.wait_ge(*s1_used(n - 1))
                    e.activation(s1[0:np_, n % 2], ps[0:np_, 6 + n % 2, :], ACT.Copy).then_inc(sc_done.sem, 1)
                for t, np_ in TILES:
                    e.wait_ge(*diff_done(t + 1))
                    e.activation(gd[0:np_, t], gd[0:np_, t], ACT.Exp).then_inc(gexp_done.sem, 1)

            def dve(e):
                S_ = dve_chain

                def variance(n):
                    g, t, np_ = ITEMS[n]
                    r, v = slice(0, np_), n % 2
                    q_rows.wait(e, g, t)
                    for h in range(2):
                        ins = e.bn_stats(st[r, h], ps[r, t, h * 256:(h + 1) * 256])
                    S_(ins)
                    for h in range(2):
                        ins = e.bn_aggr(mv[r, v, h], st[r, h])
                    S_(ins)
                    if n >= 2:
                        e.wait_ge(*qn_done(n - 1))
                    e.tensor_scalar(rstd[r, v], mv[r, v, :, 1], LN_EPS, None, ALU.add).then_inc(qvar.sem, 1)

                def coefficients(n):
                    r, v = slice(0, ITEMS[n][2]), n % 2
                    e.wait_ge(*qstd(n + 1))
                    S_(e.reciprocal(rstd[r, v], rstd[r, v]))
                    e.scalar_tensor_tensor(out=shift[r, v], in0=mv[r, v, :, 0], scalar=-1.0, in1=rstd[r, v],
                                           op0=ALU.mult, op1=ALU.mult).then_inc(qcoef.sem, 1)

                def gather(n):
                    g, t, np_ = ITEMS[n]
                    e.wait_ge(*eq_used(n + 1))
                    for w, E_ in enumerate((E1, E2)):
                        ins = e.tensor_reduce(E_[0:np_, t, 2 * g * TOPK:(2 * g + 2) * TOPK],
                                              eq[0:np_, n % 2, w].rearrange("p (k b) -> p k b", b=TOPK), AX, ALU.add)
                    ins.then_inc(top_done.sem, 1)

                variance(0)
                coefficients(0)
                for n, (g, t, np_) in enumerate(ITEMS):
                    r = slice(0, np_)
                    if n < last:
                        variance(n + 1)
                    e.wait_ge(*sc_done(n + 1))
                    s = s1[r, n % 2].rearrange("p (j n) -> p j n", j=4)
                    top16(e, S_, 4, lambda j: s[:, j], lambda j: s2[r, j], lambda j: V[r, j], lambda j: Iu[r, j])
                    e.sem_inc(s1_used.sem, 1)
                    if n < last:
                        coefficients(n + 1)
                    Vv = V[r].rearrange("p (h w) k -> p h w k", w=2)
                    cv = cand[r, :, 0:TROWS * TOPK].rearrange("p h (a b) -> p h a b", b=TOPK)
                    cw = cand[r, :, TROWS * TOPK:].rearrange("p h (a b) -> p h a b", b=TCOLS)
                    for o, rows, width in ((cv, slice(0, TROWS), TOPK), (cw, slice(TROWS, TOPK), TCOLS)):
                        sh = [np_, 2, rows.stop - rows.start, width]
                        ins = e.tensor_tensor(o, Vv[:, :, 0, rows].unsqueeze(3).broadcast_to(sh),
                                              Vv[:, :, 1, 0:width].unsqueeze(2).broadcast_to(sh), ALU.add)
                    S_(ins)
                    top16(e, S_, 2, lambda h: cand[r, h], lambda h: cand2[r, h], lambda h: G[r, t, (2 * g + h) * TOPK:(2 * g + h + 1) * TOPK],
                          lambda h: Ju[r, h])
                    if n:
                        e.wait_ge(*eq_used(n))
                    e.tensor_scalar(mask[r], Ju[r], 5, 2, ALU.logical_shift_right, ALU.bitwise_and)
                    e.tensor_copy(place[r], Ju[r])
                    S_(e.tensor_copy(If[r, n % 2], Iu[r]))
                    S_(e.tensor_scalar(mask[r], mask[r], -6.0, 15.0, ALU.mult, ALU.add))
                    Iv = If[r, n % 2].rearrange("p (h w) k -> p h w k", w=2)
                    e.tensor_copy(step1[r, :, 0:1], Iv[:, :, 0, 0:1])
                    e.tensor_tensor(step1[r, :, 1:], Iv[:, :, 0, 1:], Iv[:, :, 0, 0:TOPK - 1], ALU.subtract)
                    S_(e.tensor_tensor(mask[r], Ju[r], mask[r], ALU.bitwise_and))
                    e.tensor_copy(col[r], mask[r]).then_inc(S_.sem, 1)
                    S_.n += 1
                    ev = eq[r, n % 2].rearrange("p w (h a b) -> p w h a b", h=2, a=TOPK)
                    sh = [np_, TOPK, TOPK]
                    for h in range(2):
                        e.tensor_tensor(ev[:, 0, h], place[r, h].unsqueeze(2).broadcast_to(sh),
                                        K["row_start"][r].unsqueeze(1).broadcast_to(sh), ALU.is_ge)
                    e.wait_ge(S_.sem, S_.n)
                    for h in range(2):
                        ins = e.tensor_tensor(ev[:, 1, h], K["iota"][r, 0:TOPK].unsqueeze(1).broadcast_to(sh),
                                              col[r, h].unsqueeze(2).broadcast_to(sh), ALU.is_equal)
                    ins.then_inc(eq_done.sem, 1)
                    if n:
                        gather(n - 1)
                gather(last)
                e.wait_ge(*top_done(20))
                for t, np_ in TILES:
                    v = G[0:np_, t].rearrange("p (h k) -> p h k", h=PH)
                    e.tensor_tensor(gd[0:np_, t].rearrange("p (h k) -> p h k", h=PH), v, v[:, :, 0:1].broadcast_to([np_, PH, TOPK]),
                                    ALU.subtract).then_inc(diff_done.sem, 1)
                for t, np_ in TILES:
                    v = gd[0:np_, t].rearrange("p (h k) -> p h k", h=PH)
                    e.wait_ge(*gexp_done(t + 1))
                    S_(e.tensor_reduce(gs[0:np_, t], v, AX, ALU.add))
                    S_(e.reciprocal(gs[0:np_, t], gs[0:np_, t]))
                    e.tensor_tensor(G[0:np_, t].rearrange("p (h k) -> p h k", h=PH), v, gs[0:np_, t].unsqueeze(2).broadcast_to([np_, PH, TOPK]),
                                    ALU.mult).then_inc(gates_done.sem, 1)
                e.wait_ge(*slot_ps(1))
                e.tensor_copy(slotT[:, :, 0:SEQ], ps[:, 0:3, :]).then_inc(slot_done.sem, 1)
                e.tensor_copy(slotT[:, :, SEQ:N], ps[:, 3, 0:3 * NS_TOK].rearrange("p (w n) -> p w n", w=3)).then_inc(slot_done.sem, 1)

            return sp, pe, act, dve, pool

        def top16(e, step, n, src, rest, val, idx):
            for j in range(n):
                ins = e.max(val(j)[:, 0:8], src(j))
            step(ins)
            for j in range(n):
                e.max_index(idx(j)[:, 0:8], val(j)[:, 0:8], src(j))
                ins = e.match_replace(rest(j), val(j)[:, 0:8], src(j), -3.0e38)
            step(ins)
            for j in range(n):
                ins = e.max(val(j)[:, 8:16], rest(j))
            step(ins)
            for j in range(n):
                ins = e.max_index(idx(j)[:, 8:16], val(j)[:, 8:16], rest(j))
            step(ins)

        def stage_gates(l):
            A = Arena(arena_buf, arena_w)
            slotT = A(3, N)
            cur = A(2, 3, 32)
            oh1, oh2 = A(4, 4, NK), A(4, 4, NK)
            gb = A(2, NK * 32)
            cur_done, oh1_done, oh2_done, oh_read, g_out = (mark(*s) for s in (
                ("slot_cur", NBLK), ("onehot1", 4 * NBLK), ("onehot2", 8 * NBLK), ("onehots_read", 8 * NBLK + 4), ("G_copied", 8 * NBLK + 8)))
            stored = [mark(f"G_stored{i}", 16 * ((NBLK + 1 - i) // 2 + 1)) for i in range(2)]

            def over_blocks(e, body):
                with e.Fori(0, NBLK // 2) as i:
                    for u in range(2):
                        body(i, u)
                body(NBLK // 2, 0)

            def pe(e):
                def body(i, u):
                    for q in range(8):
                        g = i * 16 + (8 * u + q)
                        if q % 2:
                            e.wait_ge(*oh1_done(i * 8 + (4 * u + q // 2 + 1)))
                        e.wait_ge(*oh2_done(g + 1))
                        e.wait_ge(*g_out(g + 1))
                        for k in range(4):
                            mm = e.matmul(ps[:, q, k * NK:(k + 1) * NK], oh1[:, q % 4, k], oh2[:, q % 4, k], start=True, stop=True)
                        mm.then_inc(oh_read.sem, 1)
                over_blocks(e, body)

            def pool(e):
                e.sem_inc(oh_read.sem, 4)

                def body(i, u):
                    e.wait_ge(*cur_done(i * 2 + (u + 1)))
                    for q in range(1, 8, 2):
                        g = i * 16 + (8 * u + q)
                        e.wait_ge(*oh_read(g + 1))
                        alone(e)
                        for k in range(4):
                            c = 4 * q + k
                            ins = e.tensor_scalar(oh1[:, q % 4, k], K["iota"], cur[:, u, 0, c:c + 1], None, ALU.is_equal)
                        ins.then_inc(oh1_done.sem, 1)
                over_blocks(e, body)

            def dve(e):
                e.wait_ge(*oh_read(4))

                def body(i, u):
                    b = i * 2 + u
                    e.tensor_copy(cur[:, u], slotT[:, :, bass.ds(b * 32, 32)]).then_inc(cur_done.sem, 1)
                    e.wait_ge(*cur_done(b + 1))
                    for q in range(8):
                        g = i * 16 + (8 * u + q)
                        e.wait_ge(*oh_read(g + 1))
                        if q % 2 == 0:
                            sh = [P, 4, NK]
                            e.tensor_tensor(oh1[:, q % 4], K["iota"].unsqueeze(1).broadcast_to(sh),
                                            cur[:, u, 0, 4 * q:4 * q + 4].unsqueeze(2).broadcast_to(sh), ALU.is_equal)
                        for k in range(4):
                            c = 4 * q + k
                            ins = e.tensor_scalar(oh2[:, q % 4, k], K["iota"], cur[:, u, 1, c:c + 1], cur[:, u, 2, c:c + 1],
                                                  ALU.is_equal, ALU.mult)
                        ins.then_inc(oh2_done.sem, 1)
                over_blocks(e, body)

            def act(e):
                e.sem_inc(g_out.sem, 8)
                for u in range(2):
                    e.sem_inc(stored[u].sem, 16)

                def body(i, u):
                    e.wait_ge(*stored[u](i * 16 + 16))
                    for q in range(8):
                        g = i * 16 + (8 * u + q)
                        e.wait_ge(*oh_read(g + 5))
                        o = gb[:, u].rearrange("p (i n) -> p n i", n=32)[:, 4 * q:4 * q + 4]
                        e.activation(o, ps[:, q, :].rearrange("p (n i) -> p n i", n=4), ACT.Copy).then_inc(g_out.sem, 1)
                    e.wait_ge(*g_out(i * 16 + (8 * u + 16)))
                    e.dma_start(d["G"][bass.ds(i * 2 + u, 1)].rearrange("b p c -> (b p) c"), gb[:, u]).then_inc(stored[u].sem, 16)
                over_blocks(e, body)
                for u in range(2):
                    e.wait_ge(*stored[u](16 * (1 + (NBLK + 1 - u) // 2)))

            return lambda e: None, pe, act, dve, pool

        def stage_experts(l):
            A = Arena(arena_buf, exp_w)
            Y = A(KC, N)
            gel = A(2, N)
            gt = A(NBLK, TPG * 32)
            turns = NK // TPG
            base = reserve(turns * RING)
            order = [("u", 0), ("u", 1), ("u", 2), ("u", 3), ("v", 0), ("v", 1), ("v", 2), ("v", 3)]
            assert len(order) == RING and TPG == 4
            g_in, h_ps, h_read, a_hi_done, a_done, y_ps, y_read, y_zero = (mark(*s) for s in (
                ("G_in", 16 * turns), ("H_ps", TPG * turns), ("H_read", TPG * turns + 2), ("A_hi", TPG * turns), ("A_done", TPG * turns + 2),
                ("Y_ps", KC * turns + 1), ("Y_read", KC * turns + 2), ("Y_zero", 1)))
            w_hi_done, g_mul_done, h_split = mark("W_hi", RING * turns), mark("G_multiplied", TPG * turns), mark("h_split", 2)

            def parts(kind, j):
                return (uR if kind == "u" else vR)[:, j % 2 if kind == "u" else j]

            def sp(e):
                def src(i, j):
                    kind, tt = order[j]
                    t = i * TPG + tt
                    if kind == "u":
                        return d["peer_uT"][l, bass.ds(t, 1)].rearrange("a p c -> (a p) c")
                    return d["peer_v"][l][:, bass.ds(t * D, D)]
                ring.load_loop(e, src, 0, turns)

            def pe(e):
                def hidden(i, o, tt):
                    hi, lo = parts("u", tt)[:, 0], parts("u", tt)[:, 1]
                    e.wait_ge(used, i * RING + (o * RING + base + order.index(("u", tt)) + 1))
                    e.wait_ge(*h_read(i * TPG + (o * TPG + tt + 1)))
                    for h in range(2):
                        c = slice(h * HALF, (h + 1) * HALF)
                        for k in range(KC):
                            m = slice(k * P, (k + 1) * P)
                            for n, (w, v) in enumerate(((hi, 0), (hi, 1), (lo, 0))):
                                mm = e.matmul(ps[:, 2 * (tt % 2) + h, 0:HALF], w[:, m], hR[:, v, k, c],
                                              start=(k == 0 and n == 0), stop=(k == KC - 1 and n == 2))
                    mm.then_inc(h_ps.sem, 1)

                def output(i, o):
                    e.wait_ge(used, i * RING + (o * RING + base + order.index(("v", TPG - 1)) + 1))
                    e.wait_ge(*a_done(i * TPG + (o * TPG + TPG + 2)))
                    for m in range(KC):
                        e.wait_ge(*y_read(i * KC + (o * KC + m + 1)))
                        rows = slice(m * P, (m + 1) * P)
                        for h in range(2):
                            c = slice(h * HALF, (h + 1) * HALF)
                            for tt in range(TPG):
                                hi, lo = parts("v", tt)[:, 0], parts("v", tt)[:, 1]
                                for n, (w, v) in enumerate(((hi, 0), (hi, 1), (lo, 0))):
                                    mm = e.matmul(ps[:, 4 + 2 * (m % 2) + h, 0:HALF], w[:, rows], aR[:, v, tt, c],
                                                  start=(tt == 0 and n == 0), stop=(tt == TPG - 1 and n == 2))
                        mm.then_inc(y_ps.sem, 1)

                e.sem_inc(y_ps.sem, 1)
                e.wait_ge(*h_split(2))
                for tt in range(TPG):
                    hidden(0, 0, tt)
                with e.Fori(0, turns - 1) as i:
                    hidden(i, 1, 0)
                    hidden(i, 1, 1)
                    output(i, 0)
                    hidden(i, 1, 2)
                    hidden(i, 1, 3)
                output(turns - 1, 0)
                ring.taken += turns * RING

            def act(e):
                e.sem_inc(h_read.sem, 2)
                e.activation(hR[:, 0], hT, ACT.Copy).then_inc(h_split.sem, 1)

                def hi_part(i, o, j):
                    n = base + j
                    e.wait_ge(ring.landed[n % RING], i * 16 + 16 * (o + n // RING + 1))
                    e.activation(parts(*order[j])[:, 0], ring_buf[:, n % RING, :], ACT.Copy).then_inc(w_hi_done.sem, 1)

                def gelu(i, tt):
                    e.wait_ge(*h_ps(i * TPG + (tt + 1)))
                    e.wait_ge(*a_done(i * TPG + (tt + 1)))
                    e.activation(halves(gel[:, tt % 2]), pair(2 * (tt % 2)), ACT.Gelu).then_inc(h_read.sem, 1)

                def a_hi(i, tt):
                    e.wait_ge(*g_mul_done(i * TPG + (tt + 1)))
                    e.activation(aR[:, 0, tt], gel[:, tt % 2], ACT.Copy).then_inc(a_hi_done.sem, 1)

                def turn(i, last=False):
                    gelu(i, 0)
                    gelu(i, 1)
                    hi_part(i, 0, 2)
                    hi_part(i, 0, 3)
                    e.wait_ge(*y_ps(i * KC + 1))
                    for j in range(4, RING):
                        hi_part(i, 0, j)
                    a_hi(i, 0)
                    a_hi(i, 1)
                    for tt in (2, 3):
                        gelu(i, tt)
                        if not last:
                            hi_part(i, 1, tt - 2)
                        a_hi(i, tt)

                hi_part(0, 0, 0)
                hi_part(0, 0, 1)
                with e.Fori(0, turns - 1) as i:
                    turn(i)
                turn(turns - 1, last=True)

            def pool(e):
                def gates(i, o):
                    src = d["G"].rearrange("b p c -> p b c")[:, :, bass.ds(i * (TPG * 32) + o * (TPG * 32), TPG * 32)]
                    e.dma_start(gt, src).then_inc(g_in.sem, 16)

                def lo_part(i, o, j):
                    e.wait_ge(*w_hi_done(i * RING + (o * RING + j + 1)))
                    alone(e)
                    p = parts(*order[j])
                    e.tensor_tensor(p[:, 1], ring_buf[:, (base + j) % RING, :], p[:, 0].bitcast(F32), ALU.subtract).then_inc(used, 1)

                gates(0, 0)
                lo_part(0, 0, 0)
                lo_part(0, 0, 1)
                with e.Fori(0, turns - 1) as i:
                    for j in range(2, RING):
                        lo_part(i, 0, j)
                    for j in range(2):
                        lo_part(i, 1, j)
                    e.wait_ge(*g_mul_done(i * TPG + TPG))
                    gates(i, 1)
                for j in range(2, RING):
                    lo_part(turns - 1, 0, j)

            def dve(e):
                def multiply(i, o, tt):
                    e.wait_ge(*h_read(i * TPG + (o * TPG + tt + 3)))
                    v = lambda a: a.rearrange("p (b n) -> p b n", n=32)
                    g = v(gel[:, tt % 2])
                    e.tensor_tensor(g, g, gt[:, :, tt * 32:(tt + 1) * 32], ALU.mult).then_inc(g_mul_done.sem, 1)

                def a_lo(i, o, tt):
                    e.wait_ge(*a_hi_done(i * TPG + (o * TPG + tt + 1)))
                    e.tensor_tensor(aR[:, 1, tt], gel[:, tt % 2], aR[:, 0, tt].bitcast(F32), ALU.subtract).then_inc(a_done.sem, 1)

                def add_y(i):
                    for m in range(KC):
                        e.wait_ge(*y_ps(i * KC + (m + 2)))
                        e.tensor_tensor(halves(Y[:, m]), halves(Y[:, m]), pair(4 + 2 * (m % 2)), ALU.add).then_inc(y_read.sem, 1)

                def first_half(i, o):
                    e.wait_ge(*g_in(i * 16 + (o * 16 + 16)))
                    multiply(i, o, 0)
                    multiply(i, o, 1)

                def second_half(i, o):
                    a_lo(i, o, 0)
                    a_lo(i, o, 1)
                    for tt in (2, 3):
                        multiply(i, o, tt)
                        a_lo(i, o, tt)

                e.sem_inc(y_read.sem, 2)
                e.sem_inc(a_done.sem, 2)
                e.wait_ge(*h_split(1))
                e.tensor_tensor(hR[:, 1], hT, hR[:, 0].bitcast(F32), ALU.subtract).then_inc(h_split.sem, 1)
                e.memset(Y.rearrange("p k n -> p (k n)"), 0.0).then_inc(y_zero.sem, 1)
                e.wait_ge(*y_zero(1))
                first_half(0, 0)
                second_half(0, 0)
                with e.Fori(0, turns - 1) as i:
                    first_half(i, 1)
                    add_y(i)
                    second_half(i, 1)
                add_y(turns - 1)

            return sp, pe, act, dve, pool

        def stage_latent():
            A = Arena(arena_buf, arena_w)
            ckvT, krT = A(2, N), A(N)
            wuv = A(2, MH, P)
            qs, qrs = A(2, DEC_B, MH * DEC_T), A(DEC_B, MH * DEC_T)
            kept = A.at
            small = A(8, 4)
            cq = A(NT, QLORA)
            cqT = A(QC, N)
            gq, gkv = A(QLORA), A(KVL)
            qn, qlat, qr = A(N), A(2, 2, N), A(2, 2, N)
            junk = A(512)
            ckv, kr = A(NT, KVL), A(NT, DR)
            wuk = A(MH, KVL)
            prob, pT = A(2, 512), A(2, 512)
            ropef, ropet = A(2, N), A(2, NT, DR)
            t1, t2 = A(N), A(N)
            ss, var, rstd = A(NT, 3), A(NT, 2), A(NT, 2)
            krr = A(NT, DR)
            base = reserve(9)
            lat_rows = RowProduct(2, base)
            rows_in, ss_done, raw_done = sem("mla_rows_in"), sem("sumsq_done"), sem("raw_done")
            rvar, rstd_done, norm_done, lat_out = sem("rms_var"), sem("rms_std"), sem("latents_done"), sem("latents_out")
            cT_ps, cT_done = sem("latT_ps"), sem("latT_done")

            def sp(e):
                for s in range(9):
                    src = d["mla_win"][s]
                    ring.load(e, src if s < 8 else src[:, 0:KC * DR])

            def pool(e):
                e.dma_start(gq, d["mla_g_q"].broadcast_to([P, QLORA])).then_inc(rows_in, 16)
                e.dma_start(gkv, d["mla_g_kv"].broadcast_to([P, KVL])).then_inc(rows_in, 16)
                e.dma_start(wuk, d["wukT"]).then_inc(rows_in, 16)
                e.dma_start(wuv, d["wuv"]).then_inc(rows_in, 16)
                e.dma_start(ropef, d["rope_feat"]).then_inc(rows_in, 16)
                e.dma_start(ropet, d["rope_tok"]).then_inc(rows_in, 16)
                for t, np_ in TILES:
                    e.wait_ge(norm_done, t + 1)
                    r = slice(t * P, t * P + np_)
                    e.dma_start(d["o_ckv"][r], ckv[0:np_, t]).then_inc(lat_out, 16)
                    e.dma_start(d["o_kr"][r], krr[0:np_, t]).then_inc(lat_out, 16)
                e.wait_ge(lat_out, 160)

            def pe(e):
                for g in range(2):
                    def bank_free(t):
                        if g and t >= 3:
                            e.wait_ge(raw_done, t - 2)
                    lat_rows.group(e, hT, lambda t: (5 * g + t) % 8, bank_free)
                slot = ring.take(e)
                e.wait_ge(raw_done, 10)
                for t, np_ in TILES:
                    for k in range(KC):
                        mm = e.matmul(ps[0:np_, t, 0:DR], hT[:, k, cols(t, np_)], slot[:, k * DR:(k + 1) * DR],
                                      start=(k == 0), stop=(k == KC - 1))
                mm.then_inc(used, 1)
                for t, np_ in TILES:
                    e.wait_ge(norm_done, t + 1)
                    if t:
                        e.wait_ge(cT_done, t)
                    for k in range(QC):
                        transpose(e, ps[:, 5 + k // 4, (k % 4) * P:(k % 4) * P + np_], cq[0:np_, t, k * P:(k + 1) * P])
                    for k in range(2):
                        transpose(e, ps[:, 6, (2 + k) * P:(2 + k) * P + np_], ckv[0:np_, t, k * P:(k + 1) * P])
                    transpose(e, ps[0:DR, 7, 0:np_], krr[0:np_, t]).then_inc(cT_ps, 1)

            def act(e):
                for g in range(2):
                    for t, np_ in TILES:
                        lat_rows.wait(e, g, t)
                        b = (5 * g + t) % 8
                        if g or t:
                            e.wait_ge(ss_done, 5 * g + (t if g == 0 else 2 * t))
                        if g == 0:
                            e.activation(junk[0:np_], ps[0:np_, b, :], ACT.Square, accum_out=ss[0:np_, t, 0:1]).then_inc(ss_done, 1)
                        else:
                            for w in range(2):
                                e.wait_ge(ss_done, 5 + 2 * t + w)
                                e.activation(junk[0:np_, 0:256], ps[0:np_, b, w * 256:(w + 1) * 256], ACT.Square,
                                             accum_out=ss[0:np_, t, 1 + w:2 + w]).then_inc(ss_done, 1)
                e.wait_ge(rvar, 1)
                e.activation(rstd, var, ACT.Sqrt).then_inc(rstd_done, 1)
                for t, np_ in TILES:
                    e.wait_ge(cT_ps, t + 1)
                    v = ps[:, 5:7, :].rearrange("p b (k n) -> p (b k) n", k=4)
                    e.activation(cqT[:, :, cols(t, np_)], v[:, 0:QC, 0:np_], ACT.Copy)
                    e.activation(ckvT[:, :, cols(t, np_)], v[:, QC:QC + 2, 0:np_], ACT.Copy)
                    e.activation(krT[0:DR, cols(t, np_)], ps[0:DR, 7, 0:np_], ACT.Copy).then_inc(cT_done, 1)

            def dve(e):
                S_ = dve_chain
                S_(e.memset(var, 1.0))
                e.wait_ge(rows_in, 96)
                for g in range(2):
                    for t, np_ in TILES:
                        e.wait_ge(ss_done, t + 1 if g == 0 else 5 + 2 * (t + 1))
                        b = (5 * g + t) % 8
                        if g == 0:
                            e.tensor_copy(cq[0:np_, t, 0:512], ps[0:np_, b, :]).then_inc(raw_done, 1)
                        else:
                            S_(e.tensor_copy(cq[0:np_, t, 512:768], ps[0:np_, b, 0:256]))
                            e.tensor_copy(ckv[0:np_, t], ps[0:np_, b, 256:512]).then_inc(raw_done, 1)
                            S_(e.tensor_tensor(ss[0:np_, t, 0:1], ss[0:np_, t, 0:1], ss[0:np_, t, 1:2], ALU.add))
                            e.tensor_scalar(var[0:np_, t, 0:1], ss[0:np_, t, 0:1], 1.0 / QLORA, RMS_EPS, ALU.mult, ALU.add)
                            S_(e.tensor_scalar(var[0:np_, t, 1:2], ss[0:np_, t, 2:3], 1.0 / KVL, RMS_EPS, ALU.mult, ALU.add))
                e.wait_ge(raw_done, 10)
                e.sem_inc(rvar, 1)
                e.wait_ge(used, base + 9)
                for t, np_ in TILES:
                    S_(e.tensor_copy(kr[0:np_, t], ps[0:np_, t, 0:DR]))
                e.wait_ge(rstd_done, 1)
                S_(e.reciprocal(rstd, rstd))
                for t, np_ in TILES:
                    r = slice(0, np_)
                    S_(e.scalar_tensor_tensor(out=cq[r, t], in0=cq[r, t], scalar=rstd[r, t, 0:1], in1=gq[r], op0=ALU.mult, op1=ALU.mult))
                    S_(e.scalar_tensor_tensor(out=ckv[r, t], in0=ckv[r, t], scalar=rstd[r, t, 1:2], in1=gkv[r], op0=ALU.mult, op1=ALU.mult))
                    hf = DR // 2
                    e.tensor_tensor(t2[r, 0:hf], kr[r, t, hf:DR], ropet[r, 1, t, 0:hf], ALU.mult)
                    e.tensor_tensor(t2[r, hf:DR], kr[r, t, 0:hf], ropet[r, 1, t, hf:DR], ALU.mult)
                    S_(e.tensor_tensor(t1[r, 0:DR], kr[r, t], ropet[r, 0, t], ALU.mult))
                    e.tensor_tensor(krr[r, t], t1[r, 0:DR], t2[r, 0:DR], ALU.add).then_inc(norm_done, 1)

            stages.append((sp, pe, act, dve, pool))

            hbase = reserve(MH + MH // 2)
            hslot = lambda h: hbase + h + h // 2 + 1
            qn_done, ql_ps, ql_done, rp_done = sem("qnope_done"), sem("qlat_ps"), sem("qlat_done"), sem("qrope_done")
            sc_ps, nmax_done, p_done, pn_done = sem("att_scores"), sem("att_nmax"), sem("att_exp"), sem("att_prob")
            pT_ps, pT_done, ol_ps, ol_done, uv_ps, uv_done = (sem(s) for s in (
                "att_pT_ps", "att_pT", "olat_ps", "olat_done", "uv_ps", "uv_done"))
            olat = A(2, 2, SEQ)

            def sp2(e):
                for h in range(MH):
                    if h % 2 == 0:
                        ring.load(e, d["wuq_rope"][h // 2])
                    ring.load(e, d["wuq_nope"][h])

            def pe2(e):
                def project(slot, b):
                    for h2 in range(2):
                        for k in range(QC):
                            mm = e.matmul(ps[:, b + h2, 0:HALF], slot[:, k * P:(k + 1) * P], cqT[:, k, h2 * HALF:(h2 + 1) * HALF],
                                          start=(k == 0), stop=(k == QC - 1))
                    mm.then_inc(used, 1)

                def finish(n):
                    h, i = divmod(n, 4)
                    e.wait_ge(pn_done, n + 1)
                    if n:
                        e.wait_ge(pT_done, n)
                    for j in range(i + 1):
                        mm = transpose(e, ps[:, 2, j * P:(j + 1) * P], prob[:, n % 2, j * P:(j + 1) * P])
                    mm.then_inc(pT_ps, 1)
                    e.wait_ge(pT_done, n + 1)
                    if n:
                        e.wait_ge(ol_done, n)
                    for c in range(2):
                        for j in range(i + 1):
                            mm = e.matmul(ps[:, 3, c * P:(c + 1) * P], ckv[:, j, c * P:(c + 1) * P], pT[:, n % 2, j * P:(j + 1) * P],
                                          start=(j == 0), stop=(j == i))
                    mm.then_inc(ol_ps, 1)

                def values(h):
                    e.wait_ge(ol_done, 4 * (h + 1))
                    if h:
                        e.wait_ge(uv_done, h)
                    for c in range(2):
                        mm = e.matmul(ps[:, 4, :], wuv[:, c, h], olat[:, h % 2, c], start=(c == 0), stop=(c == 1))
                    mm.then_inc(uv_ps, 1)

                for h in range(MH):
                    if h % 2 == 0:
                        slot = ring.take(e)
                        if h:
                            e.wait_ge(ql_done, 2 * h)
                        project(slot, 5)
                        e.wait_ge(rp_done, h // 2 + 1)
                    slot = ring.take(e)
                    if h % 2:
                        e.wait_ge(ql_done, 2 * h)
                    project(slot, 5)
                    e.wait_ge(qn_done, h + 1)
                    for c in range(2):
                        if c:
                            e.wait_ge(ql_done, 2 * h + 1)
                        for h2 in range(2):
                            mm = e.matmul(ps[:, 5 + h2, 0:HALF], wuk[:, h, c * P:(c + 1) * P], qn[:, h2 * HALF:(h2 + 1) * HALF], start=True, stop=True)
                        mm.then_inc(ql_ps, 1)
                    e.wait_ge(ql_done, 2 * h + 2)
                    for i in range(4):
                        n = 4 * h + i
                        w = (i + 1) * P
                        if n >= 2:
                            e.wait_ge(p_done, n - 1)
                        o = ps[:, n % 2, 0:w]
                        for c in range(2):
                            e.matmul(o, qlat[:, h % 2, c, cols(i, P)], ckvT[:, c, 0:w], start=(c == 0), stop=False)
                        e.matmul(o, qrv(h)[:, cols(i, P)], krT[0:DR, 0:w],
                                 start=False, stop=True).then_inc(sc_ps, 1)
                        if n:
                            finish(n - 1)
                    if h:
                        values(h - 1)
                finish(4 * MH - 1)
                values(MH - 1)

            def qrv(h):
                return qr[0:DR, h % 2, (h // 2) % 2]

            def act2(e):
                for h in range(MH):
                    e.wait_ge(used, hslot(h) + 1)
                    if h:
                        e.wait_ge(ql_ps, 2 * h)
                    e.activation(halves(qn), pair(5), ACT.Copy).then_inc(qn_done, 1)
                    for c in range(2):
                        e.wait_ge(ql_ps, 2 * h + c + 1)
                        if h >= 2 and c == 0:
                            e.wait_ge(sc_ps, 4 * (h - 1))
                        e.activation(halves(qlat[:, h % 2, c]), pair(5), ACT.Copy).then_inc(ql_done, 1)
                    for i in range(4):
                        n = 4 * h + i
                        w = (i + 1) * P
                        e.wait_ge(nmax_done, n + 1)
                        e.activation(prob[:, n % 2, 0:w], ps[:, n % 2, 0:w], ACT.Exp, bias=small[:, 1 + n % 2, 0:1], scale=MSCALE,
                                     accum_out=small[:, 3 + n % 2, 0:1]).then_inc(p_done, 1)
                        m = n - 1
                        if m >= 0:
                            copy_pT(e, m)
                copy_pT(e, 4 * MH - 1)

            def copy_pT(e, m):
                w = (m % 4 + 1) * P
                e.wait_ge(pT_ps, m + 1)
                e.activation(pT[:, m % 2, 0:w], ps[:, 2, 0:w], ACT.Copy).then_inc(pT_done, 1)

            def dve2(e):
                S_ = dve_chain

                def rope_pair(hp):
                    e.wait_ge(used, hslot(2 * hp))
                    if hp:
                        e.wait_ge(ql_done, 4 * hp)
                    if hp >= 2:
                        e.wait_ge(sc_ps, 8 * (hp - 1))
                    src = pair(5)
                    for q in range(4):
                        a, b = slice(32 * q, 32 * q + 32), slice(32 * (q ^ 1), 32 * (q ^ 1) + 32)
                        ins = e.tensor_tensor(halves(t2[a]), src[b], halves(ropef[b, 1]), ALU.mult)
                    S_(ins)
                    S_(e.tensor_tensor(halves(t1), src, halves(ropef[:, 0]), ALU.mult))
                    for u in range(2):
                        r = slice(DR * u, DR * (u + 1))
                        ins = e.tensor_tensor(qr[0:DR, u, hp % 2], t1[r], t2[r], ALU.add)
                        if u == 0:
                            S_(ins)
                    ins.then_inc(rp_done, 1)
                    e.wait_ge(rp_done, hp + 1)

                def after(m):
                    e.wait_ge(ol_ps, m + 1)
                    if m % 4 == 0 and m >= 8:
                        e.wait_ge(uv_ps, m // 4 - 1)
                    v = ps[:, 3, 0:2 * P].rearrange("p (c n) -> p c n", c=2)
                    e.tensor_copy(olat[:, (m // 4) % 2, :, cols(m % 4, P)], v).then_inc(ol_done, 1)

                def out_values(h):
                    e.wait_ge(uv_ps, h + 1)
                    e.tensor_copy(hT[:, h, 0:SEQ], ps[:, 4, :]).then_inc(uv_done, 1)

                for h in range(MH):
                    if h % 2 == 0:
                        rope_pair(h // 2)
                    e.wait_ge(ql_done, 2 * h + 2)
                    hs = slice(h * DEC_T, (h + 1) * DEC_T)
                    e.tensor_copy(qs[:, :, :, hs], qlat[:, h % 2, :, SEQ:N].rearrange("p c (s t) -> p c s t", t=DEC_T))
                    S_(e.tensor_copy(qrs[0:DR, :, hs], qrv(h)[:, SEQ:N].rearrange("p (s t) -> p s t", t=DEC_T)))
                    for i in range(4):
                        n = 4 * h + i
                        w = (i + 1) * P
                        s = ps[:, n % 2]
                        e.wait_ge(sc_ps, n + 1)
                        S_(e.tensor_tensor(s[:, w - P:w], s[:, w - P:w], K["causal"], ALU.add))
                        S_(e.tensor_reduce(small[:, 0, 0:1], s[:, 0:w], AX, ALU.max))
                        if n >= 2:
                            e.wait_ge(p_done, n - 1)
                        e.tensor_scalar(small[:, 1 + n % 2, 0:1], small[:, 0, 0:1], -MSCALE, None, ALU.mult).then_inc(nmax_done, 1)
                        if n:
                            after(n - 1)
                        e.wait_ge(p_done, n + 1)
                        S_(e.reciprocal(small[:, 5 + n % 2, 0:1], small[:, 3 + n % 2, 0:1]))
                        e.tensor_scalar(prob[:, n % 2, 0:w], prob[:, n % 2, 0:w], small[:, 5 + n % 2, 0:1], None, ALU.mult).then_inc(pn_done, 1)
                    if h:
                        out_values(h - 1)
                after(4 * MH - 1)
                out_values(MH - 1)

            stages.append((sp2, pe2, act2, dve2, lambda e: None))

            B = Arena(arena_buf, arena_w)
            B.at = kept
            keys, vals = B(2, NPAGE, 3 * P), B(2, NPAGE, KVL)
            pr, prT, prnT = B(2, 17 * P), B(2, NPAGE * 32), B(2, 32)
            qcur, cur_new, cur_c = B(2, 3, 32), B(2, 3, DEC_T), B(2, KVL)
            sm = B(2, 8, 4)
            ol = B(DEC_B, KVL)
            new_c = ol[32:32 + DEC_T]
            olS = pr.rearrange("p v n -> p (v n)")[:, 0:2 * MH * NS_TOK].rearrange("p (c h n) -> p c h n", c=2, h=MH)
            table = B(P).bitcast(I32)
            table_in, new_in = sem("page_table_in"), sem("new_latents_in")
            keys_of, vals_of = [sem(f"page_keys_in{u}") for u in range(2)], [sem(f"page_values_in{u}") for u in range(2)]
            cur_done, s_ps, s_nmax, s_exp, s_prob, s_pT_ps, s_pT, s_ol, s_ol_done = (sem("smp_" + s) for s in (
                "cur", "scores", "nmax", "exp", "prob", "pT_ps", "pT", "olat_ps", "olat"))
            u_ps, u_done = sem("smp_uv_ps"), sem("smp_uv")

            def sweep(e, front, back):
                front(0, 0)
                with e.Fori(0, DEC_B // 2 - 1) as i:
                    for u in (1, 2):
                        front(i, u)
                        back(i, u - 1)
                last = DEC_B // 2 - 1
                front(last, 1)
                back(last, 0)
                back(last, 1)

            def sp3(e):
                e.wait_ge(stage_over, 4 * page_stage[0])
                e.dma_start(table[0:1], d["page_table"]).then_inc(table_in, 16)
                e.wait_ge(table_in, 16)
                with e.register("page") as reg:
                    with e.Fori(0, DEC_B // 2) as i:
                        for u in range(2):
                            for buf, src, landed, freed in ((keys, d["page_keys"], keys_of[u], s_ps), (vals, d["page_values"], vals_of[u], s_ol)):
                                e.wait_ge(freed, i * 2 + (u + 1))
                                alone(e)
                                for q in range(NPAGE):
                                    e.reg_load(reg, table[0:1, bass.ds((i * 2 + u) * NPAGE + q, 1)])
                                    pg = e.snap(reg, min_val=0, max_val=src.shape[0] - 1)
                                    e.dma_start(buf[:, u, q], src[bass.ds(pg, 1)].rearrange("a p n -> (a p) n")).then_inc(landed, 16)

            def pool3(e):
                e.dma_start(new_c, d["o_ckv"][SEQ:N].rearrange("(s t) c -> t s c", t=DEC_T)).then_inc(new_in, 16)

            def pe3(e):
                def scores(i, u):
                    v = u % 2
                    e.wait_ge(cur_done, i * 2 + (u + 1))
                    e.wait_ge(s_exp, i * 2 + (u + 1))
                    e.wait_ge(keys_of[v], (i + u // 2) * (16 * NPAGE) + 16 * NPAGE)
                    for w in range(4):
                        for k in range(3):
                            r = P if k < 2 else DR
                            e.matmul(ps[0:32, w, :].rearrange("p (q n) -> p q n", n=P), qcur[0:r, v, k],
                                     keys[0:r, v, 4 * w:4 * w + 4, k * P:(k + 1) * P], start=(k == 0), stop=(k == 2))
                    for k in range(3):
                        r = P if k < 2 else DR
                        mm = e.matmul(ps[0:32, 4, 0:DEC_T], qcur[0:r, v, k], cur_new[0:r, v, k], start=(k == 0), stop=(k == 2))
                    mm.then_inc(s_ps, 1)

                def values(i, v):
                    e.wait_ge(s_prob, i * 2 + (v + 1))
                    alone(e)
                    for q in range(NPAGE):
                        transpose(e, ps[:, 5, q * 32:(q + 1) * 32], pr[0:32, v, q * P:(q + 1) * P])
                    transpose(e, ps[0:DEC_T, 6, 0:32], pr[0:32, v, PAST:PAST + DEC_T]).then_inc(s_pT_ps, 1)
                    e.wait_ge(s_pT, i * 2 + (v + 1))
                    e.wait_ge(s_ol_done, i * 2 + (v + 1))
                    e.wait_ge(vals_of[v], i * (16 * NPAGE) + 16 * NPAGE)
                    o = ps[0:32, 7, 0:KVL]
                    for q in range(NPAGE):
                        e.matmul(o, prT[:, v, q * 32:(q + 1) * 32], vals[:, v, q], start=(q == 0), stop=False)
                    e.matmul(o, prnT[0:DEC_T, v], cur_c[0:DEC_T, v], start=False, stop=True).then_inc(s_ol, 1)

                e.sem_inc(s_ps, 2)
                e.sem_inc(s_ol, 2)
                sweep(e, scores, values)
                e.wait_ge(s_ol_done, DEC_B + 1)
                for b in range(DEC_B):
                    for c in range(2):
                        o = (c * DEC_B + b) * 32
                        mm = transpose(e, ps[:, 5, o:o + 32], ol[0:32, b, c * P:(c + 1) * P])
                mm.then_inc(s_pT_ps, 1)
                e.wait_ge(s_pT, DEC_B + 1)
                for h in range(MH):
                    for c in range(2):
                        mm = e.matmul(ps[:, 0, h * 32:(h + 1) * 32], wuv[:, c, h], olS[:, c, h], start=(c == 0), stop=(c == 1))
                mm.then_inc(u_ps, 1)

            def act3(e):
                e.sem_inc(s_exp, 1)
                with e.Fori(0, DEC_B // 2) as i:
                    for v in range(2):
                        b = i * 2 + v
                        e.wait_ge(s_nmax, b + 1)
                        e.activation(pr[0:32, v, 0:PAST], ps[0:32, 0:4, :].rearrange("p b n -> p (b n)"), ACT.Exp, bias=sm[0:32, v, 1, 0:1],
                                     scale=MSCALE, accum_out=sm[0:32, v, 2, 0:1])
                        e.activation(pr[0:32, v, PAST:PAST + DEC_T], sm[0:32, v, 0, 0:DEC_T], ACT.Exp, bias=sm[0:32, v, 1, 0:1], scale=MSCALE,
                                     accum_out=sm[0:32, v, 3, 0:1]).then_inc(s_exp, 1)

            def dve3(e):
                S_ = sem("sample_step")
                e.sem_inc(s_ol_done, 1)
                e.wait_ge(new_in, 16)

                def own_tokens(i, u):
                    v, b = u % 2, i * 2 + u
                    one = bass.ds(b, 1)
                    e.tensor_copy(qcur[:, v, 0:2], qs[:, :, one].rearrange("p c s n -> p c (s n)"))
                    e.tensor_copy(qcur[0:DR, v, 2], qrs[0:DR, one].rearrange("p s n -> p (s n)"))
                    own = bass.ds(b * DEC_T + SEQ, DEC_T)
                    e.tensor_copy(cur_new[:, v, 0:2], ckvT[:, :, own])
                    e.tensor_copy(cur_new[0:DR, v, 2], krT[0:DR, own])
                    e.tensor_copy(cur_c[0:DEC_T, v], new_c[:, one].rearrange("p s c -> p (s c)")).then_inc(cur_done, 1)

                def maximum(i, u):
                    v, b = u % 2, i * 2 + u
                    at = lambda n: b * 5 + n
                    s = sm[0:32, v]
                    e.wait_ge(s_ps, b + 3)
                    e.tensor_reduce(s[:, 4, 0:1], ps[0:32, 0:4, :].rearrange("p b n -> p (b n)"), AX, ALU.max)
                    e.tensor_tensor(s[:, 0, 0:DEC_T], ps[0:32, 4, 0:DEC_T], K["causal_s"][0:32], ALU.add).then_inc(S_, 1)
                    e.wait_ge(S_, at(1))
                    e.tensor_reduce(s[:, 4, 1:2], s[:, 0, 0:DEC_T], AX, ALU.max).then_inc(S_, 1)
                    e.wait_ge(S_, at(2))
                    e.tensor_reduce(s[:, 4, 2:3], s[:, 4, 0:2], AX, ALU.max).then_inc(S_, 1)
                    e.wait_ge(S_, at(3))
                    e.tensor_scalar(s[:, 1, 0:1], s[:, 4, 2:3], -MSCALE, None, ALU.mult).then_inc(s_nmax, 1)

                def normalise(i, u):
                    v, b = u % 2, i * 2 + u
                    at = lambda n: b * 5 + n
                    s = sm[0:32, v]
                    e.wait_ge(s_exp, b + 2)
                    e.tensor_tensor(s[:, 5, 0:1], s[:, 2, 0:1], s[:, 3, 0:1], ALU.add).then_inc(S_, 1)
                    e.wait_ge(S_, at(4))
                    e.reciprocal(s[:, 6, 0:1], s[:, 5, 0:1]).then_inc(S_, 1)
                    e.wait_ge(S_, at(5))
                    e.tensor_scalar(pr[0:32, v, 0:PAST + DEC_T], pr[0:32, v, 0:PAST + DEC_T], s[:, 6, 0:1], None, ALU.mult).then_inc(s_prob, 1)

                def probs_out(i, v):
                    e.wait_ge(s_pT_ps, i * 2 + (v + 1))
                    e.tensor_copy(prT[:, v], ps[:, 5, :])
                    e.tensor_copy(prnT[0:DEC_T, v], ps[0:DEC_T, 6, 0:32]).then_inc(s_pT, 1)

                def values_out(i, v):
                    b = i * 2 + v
                    e.wait_ge(s_ol, b + 3)
                    e.tensor_copy(ol[0:32, bass.ds(b, 1)].rearrange("p b c -> p (b c)"), ps[0:32, 7, 0:KVL]).then_inc(s_ol_done, 1)

                def front(i, u):
                    own_tokens(i, u)
                    maximum(i, u)
                    if u:
                        probs_out(i, u - 1)
                    normalise(i, u)

                def back(i, v):
                    if v == 1 and isinstance(i, int):
                        probs_out(i, v)
                    values_out(i, v)

                sweep(e, front, back)
                e.wait_ge(s_pT_ps, DEC_B + 1)
                v = ps[:, 5, :].rearrange("p (c b h t) -> p c h b t", c=2, b=DEC_B, h=MH)
                for c in range(2):
                    ins = e.tensor_copy(olS[:, c].rearrange("p h (b t) -> p h b t", t=DEC_T), v[:, c])
                ins.then_inc(s_pT, 1)
                e.wait_ge(u_ps, 1)
                e.tensor_copy(hT[:, :, SEQ:N], ps[:, 0, 0:MH * 32].rearrange("p (h n) -> p h n", h=MH)).then_inc(u_done, 1)

            page_stage = [len(stages)]
            stages.append((sp3, pe3, act3, dve3, pool3))

        stages.append(stage_ada())
        stages.append(stage_modulate(0, 0))
        stages.append(stage_gla())
        stages.append(stage_close(0, 0, w_o="gla_wo"))

        def peer(l):
            stages.append(stage_modulate(l, 1))
            stages.append(stage_search(l))
            stages.append(stage_gates(l))
            stages.append(stage_experts(l))
            stages.append(stage_close(l, 1, yT=Arena(arena_buf, arena_w)(KC, N)))

        peer(0)
        stages.append(stage_modulate(1, 0))
        stage_latent()
        stages.append(stage_close(1, 0, w_o="mla_wo"))
        peer(1)
        y_out = sem("y_out")

        def store(e):
            for t, np_ in TILES:
                e.dma_start(d["o_y"][t * P:t * P + np_], x[0:np_, t]).then_inc(y_out, 16)
            e.wait_ge(y_out, 16 * NT)

        stages.append((lambda e: None, lambda e: None, store, lambda e: None, lambda e: None))

        def run(eng, which):
            for n, s in enumerate(stages):
                if n and which:
                    eng.wait_ge(stage_over, 4 * n)
                s[which](eng)
                if which:
                    eng.drain().then_inc(stage_over, 1)

        block = ctx.enter_context(nc.Block())

        @block.sync
        def _(sp):
            run(sp, 0)

        @block.tensor
        def _(pe):
            run(pe, 1)

        @block.scalar
        def _(act):
            run(act, 2)

        @block.vector
        def _(dve):
            run(dve, 3)

        @block.gpsimd
        def _(pool):
            run(pool, 4)


def kernel(x_prompt, x_sample, c_prompt, c_sample, cache_ckv, cache_krope, state_gla, page_table, ada_w, ada_b,
           ln_g, ln_b, gla_w_in, gla_w_g2, gla_b_g, gla_norm_g, gla_w_o, mla_w_in, mla_g_q, mla_g_kv, mla_w_uq,
           mla_w_uk, mla_w_uv, mla_w_o, peer_w_q, peer_k1, peer_k2, peer_u, peer_v):
    import concourse.bacc as bacc
    from concourse.bass_utils import run_bass_kernel_spmd

    a = {k: np.asarray(v) for k, v in dict(locals()).items() if k not in ("bacc", "run_bass_kernel_spmd")}
    con, rope_tok, rope_feat = constants()
    cat = np.concatenate

    def rows(w):
        return w.reshape(4, 2, P, -1, 512).transpose(3, 0, 2, 1, 4).reshape(-1, P, SLOT)

    def blocks(w):
        r = w.shape[0] // P
        return w.reshape(r, P, -1, P).transpose(2, 1, 0, 3).reshape(-1, P, r * P)

    hk, hv = GH * GDK, GH * GDV
    gw, mw = a["gla_w_in"][0], a["mla_w_in"][0]
    uq = a["mla_w_uq"][0].reshape(QLORA, MH, DN + DR)
    ins = {
        "con": con, "rope_tok": rope_tok, "rope_feat": rope_feat,
        "cT": cat([a["c_prompt"], a["c_sample"]]).T.reshape(KC, P, NSEQ).transpose(1, 0, 2).reshape(P, -1),
        "ada_w": a["ada_w"].reshape(2, KC, P, 6, D).transpose(0, 3, 1, 2, 4).reshape(-1, P, D),
        "ada_b": a["ada_b"].reshape(1, -1),
        "x": cat([a["x_prompt"].reshape(SEQ, D), a["x_sample"].reshape(NS_TOK, D)]),
        "ln_g": a["ln_g"].reshape(4, D), "ln_b": a["ln_b"].reshape(4, D),
        "gla_w": cat([blocks(gw[:, :2 * hk]), rows(gw[:, 2 * hk:2 * hk + 2 * hv])]),
        "gla_wgl": gw[:, 2 * hk + 2 * hv:].reshape(KC, P, 16).transpose(1, 0, 2).reshape(P, -1),
        "gla_wg2": cat([a["gla_w_g2"][0], a["gla_b_g"]]),
        "gla_norm_g": a["gla_norm_g"],
        "gla_wo": rows(a["gla_w_o"][0]),
        "state_gla": a["state_gla"][0],
        "mla_win": cat([rows(mw[:, :1024]), np.pad(mw[:, 1024:].reshape(KC, P, DR).transpose(1, 0, 2).reshape(1, P, -1),
                                                   ((0, 0), (0, 0), (0, SLOT - KC * DR)))]),
        "mla_g_q": a["mla_g_q"], "mla_g_kv": a["mla_g_kv"],
        "wuq_nope": blocks(uq[:, :, :DN].reshape(QLORA, -1)), "wuq_rope": blocks(uq[:, :, DN:].reshape(QLORA, -1)),
        "wukT": a["mla_w_uk"][0].transpose(2, 1, 0).reshape(P, -1),
        "wuv": a["mla_w_uv"][0].reshape(2, P, MH * P).transpose(1, 0, 2).reshape(P, -1),
        "mla_wo": rows(a["mla_w_o"][0]),
        "page_keys": cat([a["cache_ckv"][0].reshape(-1, PAGE, 2, P).transpose(0, 3, 2, 1).reshape(-1, P, 2 * PAGE),
                          np.pad(a["cache_krope"][0].transpose(0, 2, 1), ((0, 0), (0, P - DR), (0, 0)))], -1),
        "page_values": a["cache_ckv"][0],
        "page_table": a["page_table"].reshape(1, -1),
        "peer_wq": np.stack([rows(a["peer_w_q"][l]) for l in range(2)]),
        "peer_keyT": np.stack([np.stack([a[k][l].T for k in ("peer_k1", "peer_k2")], 1).reshape(P, -1) for l in range(2)]),
        "peer_uT": a["peer_u"].reshape(2, NK, NK, KC, P).transpose(0, 2, 4, 3, 1).reshape(2, NK, P, D),
        "peer_v": a["peer_v"].reshape(2, NK, NK * D),
    }
    outs = {"o_y": (N, D), "o_gla_p": (GH, GDK, GDV), "o_gla_s": (DEC_B, GH, GDK, GDV), "o_ckv": (N, KVL), "o_kr": (N, DR)}
    nc = bacc.Bacc("TRN2", target_bir_lowering=False, num_devices=1)
    arrays, d = {}, {}
    for name, v in ins.items():
        v = np.ascontiguousarray(v)
        arrays["in_" + name] = v
        d[name] = nc.dram_tensor("in_" + name, v.shape, mybir.dt.from_np(v.dtype), kind="ExternalInput").ap()
    for name, shape in outs.items():
        d[name] = nc.dram_tensor(name, shape, F32, kind="ExternalOutput").ap()
    d["mod"] = nc.dram_tensor("mod_rows", (NSEQ, 12 * D), F32, kind="Internal").ap()
    d["G"] = nc.dram_tensor("gates_dense", (NBLK, P, NK * 32), F32, kind="Internal").ap()
    for name, k in (("cT", KC), ("gla_wgl", KC)):
        d[name] = d[name].rearrange("p (k n) -> p k n", k=k)
    d["peer_keyT"] = d["peer_keyT"].rearrange("l p (w n) -> l p w n", w=2)
    d["wukT"] = d["wukT"].rearrange("p (h c) -> p h c", h=MH)
    d["wuv"] = d["wuv"].rearrange("p (c h v) -> p c h v", c=2, h=MH)
    d["rope_feat"] = d["rope_feat"].rearrange("p (w n) -> p w n", w=2)
    d["rope_tok"] = d["rope_tok"].rearrange("p (w t n) -> p w t n", w=2, t=NT)
    build(nc, d)
    r = run_bass_kernel_spmd(nc, [arrays], core_ids=[0]).results[0]
    y, ckv, kr = r["o_y"], r["o_ckv"], r["o_kr"]
    return (y[:SEQ].reshape(1, SEQ, D), y[SEQ:].reshape(DEC_B, DEC_T, D),
            r["o_gla_p"].reshape(1, 1, GH, GDK, GDV), r["o_gla_s"].reshape(1, DEC_B, GH, GDK, GDV),
            ckv[:SEQ].reshape(1, 1, SEQ, KVL), kr[:SEQ].reshape(1, 1, SEQ, DR),
            ckv[SEQ:].reshape(1, DEC_B, DEC_T, KVL), kr[SEQ:].reshape(1, DEC_B, DEC_T, DR))
```
